# Optimizing a Trainium2 kernel written in Bass

```python
import jax, jax.numpy as jnp
from jax import lax
import numpy as np

D_MODEL = 1024
BATCH = 1
SEQ = 512
DEPTH = 1

W_BRANCH = D_MODEL
N_BRANCH = 3
POOL_WINDOWS = (2, 4, 8, 16)
N_POOL_GROUPS = len(POOL_WINDOWS)
POOL_GROUP = W_BRANCH // N_POOL_GROUPS
SHORT_CONV = 3
CONFORMER_CONV = 31
LN_EPS = 1e-5
ALPHA = (2 * DEPTH) ** 0.25
BETA = (8 * DEPTH) ** -0.25

SPLIT_SIZES = (
    W_BRANCH, W_BRANCH,
    W_BRANCH, W_BRANCH, W_BRANCH, W_BRANCH,
    W_BRANCH, W_BRANCH, W_BRANCH,
    N_BRANCH * D_MODEL,
)
IN_COLS = int(sum(SPLIT_SIZES))
SPLIT_IDX = [int(v) for v in np.cumsum(SPLIT_SIZES)[:-1]]


def layer_norm(x, g=None, b=None):
    x32 = x.astype(jnp.float32)
    mu = jnp.mean(x32, axis=-1, keepdims=True)
    var = jnp.mean(jnp.square(x32 - mu), axis=-1, keepdims=True)
    y = (x32 - mu) * lax.rsqrt(var + LN_EPS)
    if g is not None:
        y = y * g.astype(jnp.float32) + b.astype(jnp.float32)
    return y.astype(x.dtype)

def causal_dwconv(u, w, b):
    K, C = w.shape
    y = lax.conv_general_dilated(
        u, w[:, None, :].astype(u.dtype), window_strides=(1,),
        padding=[(K - 1, 0)], dimension_numbers=("NWC", "WIO", "NWC"),
        feature_group_count=C)
    return y + b

def causal_multiscale_pool(v):
    bsz, slen, _ = v.shape
    vg = v.reshape(bsz, slen, N_POOL_GROUPS, POOL_GROUP).astype(jnp.float32)
    cs = jnp.cumsum(vg, axis=1)
    t = jnp.arange(1, slen + 1, dtype=jnp.float32)
    outs = []
    for g, w in enumerate(POOL_WINDOWS):
        c_g = cs[:, :, g]
        lagged = jnp.pad(c_g, ((0, 0), (w, 0), (0, 0)))[:, :slen]
        cnt = jnp.minimum(t, float(w))[None, :, None]
        outs.append((c_g - lagged) / cnt)
    pooled = jnp.stack(outs, axis=2)
    return (pooled - vg).astype(v.dtype)

def hybrid_layer(x, c_act, w_ada, b_ada, w_in, b_in, pool_w, pool_scale, sc_w, sc_b,
                 cf_w, cf_b, cf_ln_g, cf_ln_b, w_branch, w_out, ln_g, ln_b):
    bsz, slen, _ = x.shape
    mod = (c_act @ w_ada + b_ada)[:, None, :]
    shift, scale, gate = jnp.split(mod, 3, axis=-1)
    u = layer_norm(x) * (1 + scale) + shift
    proj = u @ w_in + b_in
    a_v, a_g, b_b, b_c, b_h, b_g, c_a, c_b, c_g, merge = jnp.split(proj, SPLIT_IDX, axis=-1)

    pooled = causal_multiscale_pool(a_v)
    y_a = jnp.einsum("bsgi,gio->bsgo", pooled, pool_w).reshape(bsz, slen, W_BRANCH)
    y_a = y_a * pool_scale * jax.nn.silu(a_g)

    y_b = b_b * causal_dwconv(b_c * b_h, sc_w, sc_b) * jax.nn.silu(b_g)

    h_c = causal_dwconv(c_a * jax.nn.sigmoid(c_b), cf_w, cf_b)
    y_c = jax.nn.silu(layer_norm(h_c, cf_ln_g, cf_ln_b)) * jax.nn.silu(c_g)

    g_m = jax.nn.sigmoid(merge).reshape(bsz, slen, N_BRANCH, D_MODEL)
    m = (g_m[:, :, 0] * (y_a @ w_branch[0])
         + g_m[:, :, 1] * (y_b @ w_branch[1])
         + g_m[:, :, 2] * (y_c @ w_branch[2]))
    out = m @ w_out
    return layer_norm(ALPHA * x + gate * out, ln_g, ln_b)

def first_inputs(seed: int = 0) -> dict:
    key = jax.random.key(seed)
    ks = jax.random.split(key, 20)
    L, D, W = DEPTH, D_MODEL, W_BRANCH
    n = lambda k, shp, s: jax.random.normal(k, shp, jnp.float32) * s
    return {
        "x": n(ks[0], (BATCH, SEQ, D), 1.0),
        "c": n(ks[1], (BATCH, D), 1.0),
        "w_ada": n(ks[2], (L, D, 3 * D), 0.5 * D ** -0.5),
        "b_ada": n(ks[3], (L, 3 * D), 0.02),
        "w_in": n(ks[4], (L, D, IN_COLS), D ** -0.5),
        "b_in": n(ks[5], (L, IN_COLS), 0.02),
        "pool_w": n(ks[6], (L, N_POOL_GROUPS, POOL_GROUP, POOL_GROUP), POOL_GROUP ** -0.5),
        "pool_scale": 1.0 + n(ks[7], (L, W), 0.1),
        "sc_w": n(ks[8], (L, SHORT_CONV, W), SHORT_CONV ** -0.5),
        "sc_b": n(ks[9], (L, W), 0.02),
        "cf_w": n(ks[10], (L, CONFORMER_CONV, W), CONFORMER_CONV ** -0.5),
        "cf_b": n(ks[11], (L, W), 0.02),
        "cf_ln_g": 1.0 + n(ks[12], (L, W), 0.05),
        "cf_ln_b": n(ks[13], (L, W), 0.02),
        "w_branch": n(ks[14], (L, N_BRANCH, W, D), BETA * W ** -0.5),
        "w_out": n(ks[15], (L, D, D), BETA * D ** -0.5),
        "ln_g": 1.0 + n(ks[16], (L, D), 0.05),
        "ln_b": n(ks[17], (L, D), 0.02),
    }

def first_block(x, c, w_ada, b_ada, w_in, b_in, pool_w, pool_scale, sc_w, sc_b,
              cf_w, cf_b, cf_ln_g, cf_ln_b, w_branch, w_out, ln_g, ln_b):
    c_act = jax.nn.silu(c)
    for l in range(DEPTH):
        x = hybrid_layer(x, c_act, w_ada[l], b_ada[l], w_in[l], b_in[l], pool_w[l],
                         pool_scale[l], sc_w[l], sc_b[l], cf_w[l], cf_b[l],
                         cf_ln_g[l], cf_ln_b[l], w_branch[l], w_out[l], ln_g[l], ln_b[l])
    return x


DEPTH_2 = 2

HEAD_DIM = 64
DIL_PAIRS = ((128, 1), (512, 4), (2048, 16))
N_DIL_GROUPS = len(DIL_PAIRS)
DIL_HEADS_PER_GROUP = 4
DIL_HEADS = N_DIL_GROUPS * DIL_HEADS_PER_GROUP
SB_HEADS = 4
DIL_WIDTH = DIL_HEADS * HEAD_DIM
SB_WIDTH = SB_HEADS * HEAD_DIM
DIL_OUT_WIDTH = DIL_HEADS_PER_GROUP * HEAD_DIM
N_BRANCHES = 2
IN_COLS_2 = 3 * DIL_WIDTH + 3 * SB_WIDTH + N_BRANCHES * D_MODEL
D_FF = 2816
CONV_WIDTH = 3
ROPE_THETA = 500000.0
ROPE_DIM = HEAD_DIM // 4
Q_BLOCK = 128
NORM_EPS = 1e-5
MAX_POS_OFFSET = 4096
MASK_VALUE = -1e30


def rms_norm(x, gain):
    xf = x.astype(jnp.float32)
    xf = xf * lax.rsqrt(jnp.mean(xf * xf, axis=-1, keepdims=True) + NORM_EPS)
    return (xf * gain.astype(jnp.float32)).astype(x.dtype)

def rope_tables(positions, dtype):
    inv_freq = ROPE_THETA ** (-jnp.arange(0, ROPE_DIM, 2, dtype=jnp.float32) / ROPE_DIM)
    ang = positions.astype(jnp.float32)[..., None] * inv_freq
    return (jnp.cos(ang)[:, :, None, None, :].astype(dtype),
            jnp.sin(ang)[:, :, None, None, :].astype(dtype))

def apply_partial_rope(x, cos, sin):
    half = ROPE_DIM // 2
    x1, x2, rest = x[..., :half], x[..., half:ROPE_DIM], x[..., ROPE_DIM:]
    return jnp.concatenate([x1 * cos - x2 * sin, x2 * cos + x1 * sin, rest], axis=-1)

def dilated_attention(q, k, v):
    b, s = q.shape[0], q.shape[1]
    n_blocks = s // Q_BLOCK
    scale = HEAD_DIM ** -0.5
    qs = [q[:, :, g] for g in range(N_DIL_GROUPS)]
    ks = [k[:, :, g] for g in range(N_DIL_GROUPS)]
    vs = [v[:, :, g] for g in range(N_DIL_GROUPS)]

    def block(t0):
        t = t0 + jnp.arange(Q_BLOCK)
        outs, lses = [], []
        for g, (window, dil) in enumerate(DIL_PAIRS):
            n_keys = window // dil + 1
            idx = t[:, None] - dil * jnp.arange(n_keys)[None, :]
            valid = idx >= 0
            idx = jnp.maximum(idx, 0)
            qg = lax.dynamic_slice_in_dim(qs[g], t0, Q_BLOCK, axis=1)
            kg = ks[g][:, idx]
            vg = vs[g][:, idx]
            sc = jnp.einsum('bqhd,bqkhd->bhqk', qg, kg).astype(jnp.float32) * scale
            sc = jnp.where(valid[None, None], sc, MASK_VALUE)
            m = jnp.max(sc, axis=-1, keepdims=True)
            p = jnp.exp(sc - m)
            den = jnp.sum(p, axis=-1)
            o = jnp.einsum('bhqk,bqkhd->bqhd', p, vg.astype(jnp.float32))
            o = o / jnp.transpose(den, (0, 2, 1))[..., None]
            outs.append(o)
            lses.append(m[..., 0] + jnp.log(den))
        o_all = jnp.stack(outs, axis=0)
        w = jax.nn.softmax(jnp.stack(lses, axis=0), axis=0)
        w = jnp.transpose(w, (0, 1, 3, 2))[..., None]
        return jnp.sum(w * o_all, axis=0).astype(q.dtype)

    out = lax.map(block, jnp.arange(n_blocks) * Q_BLOCK)
    return jnp.moveaxis(out, 0, 1).reshape(b, s, DIL_OUT_WIDTH)

def stick_breaking_attention(q, k, v):
    b, s = q.shape[0], q.shape[1]
    n_blocks = s // Q_BLOCK
    scale = HEAD_DIM ** -0.5
    key_pos = jnp.arange(s)

    def block(t0):
        qb = lax.dynamic_slice_in_dim(q, t0, Q_BLOCK, axis=1)
        z = jnp.einsum('bqhd,bkhd->bhqk', qb, k).astype(jnp.float32) * scale
        t = t0 + jnp.arange(Q_BLOCK)
        causal = key_pos[None, :] < t[:, None]
        log_keep = jnp.where(causal, jax.nn.log_sigmoid(-z), 0.0)
        suffix = lax.cumsum(log_keep, axis=3, reverse=True) - log_keep
        attn = jnp.where(causal, jnp.exp(jax.nn.log_sigmoid(z) + suffix), 0.0)
        return jnp.einsum('bhqk,bkhd->bqhd', attn, v.astype(jnp.float32)).astype(q.dtype)

    out = lax.map(block, jnp.arange(n_blocks) * Q_BLOCK)
    return jnp.moveaxis(out, 0, 1).reshape(b, s, SB_WIDTH)

def conv_ffn(h, w_up, conv_w, conv_b, w_down):
    up = h @ w_up
    a, bval = up[..., :D_FF], up[..., D_FF:]
    a = lax.conv_general_dilated(a, conv_w[:, None, :].astype(a.dtype), window_strides=(1,),
                                 padding=((CONV_WIDTH - 1, 0),),
                                 dimension_numbers=('NWC', 'WIO', 'NWC'),
                                 feature_group_count=D_FF) + conv_b
    return (jax.nn.silu(a) * bval) @ w_down

def second_inputs(seed: int = 0) -> dict:
    key = jax.random.key(seed)
    ks = jax.random.split(key, 16)
    f32 = jnp.float32
    nrm = lambda k, shape, s: jax.random.normal(k, shape, f32) * s
    x = jax.random.normal(ks[0], (BATCH, SEQ, D_MODEL), f32)
    offset = jax.random.randint(ks[1], (BATCH, 1), 0, MAX_POS_OFFSET, dtype=jnp.int32)
    positions = offset + jnp.arange(SEQ, dtype=jnp.int32)[None, :]
    return {
        "x": x,
        "positions": positions,
        "norm_mix": 1.0 + nrm(ks[2], (DEPTH_2, D_MODEL), 0.05),
        "w_in": nrm(ks[3], (DEPTH_2, D_MODEL, IN_COLS_2), D_MODEL ** -0.5),
        "b_gate": nrm(ks[4], (DEPTH_2, N_BRANCHES * D_MODEL), 0.1),
        "w_proj_a": nrm(ks[5], (DEPTH_2, DIL_OUT_WIDTH, D_MODEL), DIL_OUT_WIDTH ** -0.5),
        "w_proj_b": nrm(ks[6], (DEPTH_2, SB_WIDTH, D_MODEL), SB_WIDTH ** -0.5),
        "w_out": nrm(ks[7], (DEPTH_2, D_MODEL, D_MODEL), D_MODEL ** -0.5),
        "norm_ffn": 1.0 + nrm(ks[8], (DEPTH_2, D_MODEL), 0.05),
        "w_up": nrm(ks[9], (DEPTH_2, D_MODEL, 2 * D_FF), D_MODEL ** -0.5),
        "conv_w": nrm(ks[10], (DEPTH_2, CONV_WIDTH, D_FF), CONV_WIDTH ** -0.5),
        "conv_b": nrm(ks[11], (DEPTH_2, D_FF), 0.02),
        "w_down": nrm(ks[12], (DEPTH_2, D_FF, D_MODEL), D_FF ** -0.5),
        "norm_final": 1.0 + nrm(ks[13], (D_MODEL,), 0.05),
    }

def second_block(x, positions, norm_mix, w_in, b_gate, w_proj_a, w_proj_b, w_out,
              norm_ffn, w_up, conv_w, conv_b, w_down, norm_final):
    b, s, _ = x.shape
    cos, sin = rope_tables(positions, x.dtype)
    splits = np.cumsum([DIL_WIDTH, DIL_WIDTH, DIL_WIDTH, SB_WIDTH, SB_WIDTH, SB_WIDTH]).tolist()
    for l in range(DEPTH_2):
        h = rms_norm(x, norm_mix[l])
        proj = h @ w_in[l]
        dq, dk, dv, sq, sk, sv, gate_logits = jnp.split(proj, splits, axis=-1)
        dshape = (b, s, N_DIL_GROUPS, DIL_HEADS_PER_GROUP, HEAD_DIM)
        dq = apply_partial_rope(dq.reshape(dshape), cos, sin)
        dk = apply_partial_rope(dk.reshape(dshape), cos, sin)
        dv = dv.reshape(dshape)
        sshape = (b, s, SB_HEADS, HEAD_DIM)
        y_a = dilated_attention(dq, dk, dv) @ w_proj_a[l]
        y_b = stick_breaking_attention(sq.reshape(sshape), sk.reshape(sshape), sv.reshape(sshape)) @ w_proj_b[l]
        gates = jax.nn.sigmoid(gate_logits + b_gate[l])
        mixed = gates[..., :D_MODEL] * y_a + gates[..., D_MODEL:] * y_b
        x = x + mixed @ w_out[l]
        h = rms_norm(x, norm_ffn[l])
        x = x + conv_ffn(h, w_up[l], conv_w[l], conv_b[l], w_down[l])
    return rms_norm(x, norm_final)


def setup_inputs(seed=0):
    out = dict(first_inputs(seed))
    for name, value in second_inputs(seed + 1).items():
        if name != "x":
            out[name + "_2"] = value
    return out


def reference(
    x, c, w_ada, b_ada, w_in, b_in, pool_w, pool_scale, sc_w, sc_b, cf_w, cf_b, cf_ln_g,
    cf_ln_b, w_branch, w_out, ln_g, ln_b, positions_2, norm_mix_2, w_in_2, b_gate_2, w_proj_a_2,
    w_proj_b_2, w_out_2, norm_ffn_2, w_up_2, conv_w_2, conv_b_2, w_down_2, norm_final_2,
):
    x = first_block(
        x, c, w_ada, b_ada, w_in, b_in, pool_w, pool_scale, sc_w, sc_b, cf_w, cf_b, cf_ln_g,
        cf_ln_b, w_branch, w_out, ln_g, ln_b,
    )
    return second_block(
        x, positions_2, norm_mix_2, w_in_2, b_gate_2, w_proj_a_2, w_proj_b_2, w_out_2,
        norm_ffn_2, w_up_2, conv_w_2, conv_b_2, w_down_2, norm_final_2,
    )


_drawn_inputs = setup_inputs


def setup_inputs(seed=0):
    import zlib

    import numpy as np

    out = dict(_drawn_inputs(seed))
    spreads = {}
    factors = {'b_ada': 8.0,
     'b_in': 8.0,
     'pool_scale': 8.0,
     'sc_b': 51.368,
     'cf_b': 8.0,
     'cf_ln_g': 33.461,
     'cf_ln_b': 64.0,
     'b_gate_2': 2.682,
     'conv_b_2': 4.078}
    for name, (base, spread) in spreads.items():
        noise = np.random.default_rng([zlib.crc32(name.encode()), seed]).standard_normal(out[name].shape)
        drawn = base * np.exp(spread * noise) if base else spread * noise
        out[name] = __import__('jax').numpy.asarray(drawn.astype(out[name].dtype))
    for name, factor in factors.items():
        out[name] = (out[name] * factor).astype(out[name].dtype)
    return out
```

```python
import numpy as np
from contextlib import ExitStack
import concourse.bass as bass
from concourse import mybir

P = 128
D = 1024
SEQ = 512
KT = D // P
TB = SEQ // P
LAYERS = 2
POOL_WINDOWS = (2, 4, 8, 16)
CF_TAPS = 31
SC_TAPS = 3
LN_EPS = 1e-5
ALPHA = 2.0 ** 0.25
D_FF = 2816
FT = D_FF // P
HEAD = 64
ROPE_DIM = HEAD // 4
ROPE_THETA = 500000.0
MASK = -1e30
TWO_PI = 2.0 * np.pi

VECS = [("b_in", 96), ("pool_scale", 8), ("sc_w", 24), ("sc_b", 8), ("cf_b", 8), ("cf_ln_g", 8),
        ("cf_ln_b", 8), ("c", 8), ("b_ada", 24), ("cf_w", CF_TAPS * 8), ("norm_mix", 16),
        ("b_gate", 32), ("norm_ffn", 16), ("conv_w", 2 * 3 * FT), ("conv_b", 2 * FT)]
VOFF, _n = {}, 0
for _name, _rows in VECS:
    VOFF[_name] = _n
    _n += _rows
NVEC = _n
AV, AG, BB, BC, BH, BG, CA, CB, CG, MG = (8 * i for i in range(10))

CONSTS = [("ident", 128), ("negtri", 128), ("swap", 128), ("sbmul", 128), ("corr", 64), ("freq", 1),
          ("sign", 1), ("band", 516), ("own", 256), ("sbadd", 128)]
COFF, _n = {}, 0
for _name, _rows in CONSTS:
    COFF[_name] = _n
    _n += _rows
NCONST = _n
NKEEP = COFF["band"]


def shape_constants():
    out = np.zeros((P, NCONST), np.float32)
    i = np.arange(P)

    def put(name, value):
        value = np.asarray(value, np.float32).reshape(P, -1)
        out[:, COFF[name]:COFF[name] + value.shape[1]] = value

    put("ident", np.eye(P))
    put("negtri", -(i[:, None] >= i[None, :]).astype(np.float32))
    swap = np.zeros((P, P))
    for p in range(P):
        if p % HEAD < ROPE_DIM:
            swap[p - p % ROPE_DIM + (p % ROPE_DIM + ROPE_DIM // 2) % ROPE_DIM, p] = 1.0
    put("swap", swap)
    put("sbmul", (i[:, None] < i[None, :]).astype(np.float32))
    put("sbadd", np.where(i[:, None] < i[None, :], 0.0, MASK))
    t = np.arange(16)
    put("corr", np.tile(np.concatenate([w / np.minimum(t + 1, w) for w in POOL_WINDOWS])[None], (P, 1)))
    inv = (np.float32(ROPE_THETA) ** (-np.arange(0, ROPE_DIM, 2, dtype=np.float32) / np.float32(ROPE_DIM)))
    put("freq", np.where(i % HEAD < ROPE_DIM, inv[i % (ROPE_DIM // 2)], 0.0))
    put("sign", np.where(i % ROPE_DIM < ROPE_DIM // 2, -1.0, 1.0))
    gap = 4 * i[:, None] - (np.arange(516)[None, :] - 3)
    put("band", np.where((gap >= 0) & (gap <= 128), 0.0, MASK))
    gap = i[:, None] - i[None, :]
    put("own", np.concatenate([np.where(gap >= 0, 0.0, MASK),
                               np.where((gap >= 0) & (gap % 4 == 0), 0.0, MASK)], 1))
    return out


def weight_plan():
    chunks, number = [], {}

    def add(tensor, key, keys, words):
        pieces = []
        for k in keys:
            number[k] = len(number)
            pieces.append((k, words))
        chunks.append((tensor, key, pieces))

    def cols(tensor, sec, pair):
        add(tensor, (tensor, sec, pair), [(tensor, sec + 2 * pair + j) for j in range(2)], 1024)

    for p in range(4):
        for sec in (CA, CB, CG, AV, AG):
            cols("w_in", sec, p)
        add("pool_w", ("pool_w", p), [("pool_w", p)], 512)
        for sec in (BC, BH, BB, BG):
            cols("w_in", sec, p)
    for i in range(3):
        for q in range(4):
            cols("w_in", MG + 8 * i, q)
            add("w_branch", ("w_branch", i, q), [("w_branch", i, 2 * q + j) for j in range(2)], 1024)

    def rows(tensor, l, nk):
        for half in range(2):
            for k0 in range(0, nk, 4):
                n = min(4, nk - k0)
                add(tensor, (tensor, l, half, k0, n),
                    [(tensor, l, half, k0 + 2 * j) for j in range(n // 2)], 1024)

    rows("w_out", None, KT)
    for l in range(LAYERS):
        for name, sec in (("sq", 9), ("sk", 10)):
            add("w_in_2", ("w_in_2", l, sec), [(name, l, j) for j in range(2)], 1024)
        add("w_in_2", ("w_in_2v", l, 11), [("sv", l, j) for j in range(2)], 1024)
        for name, sec in (("dq", 0), ("dk", 3)):
            for g in range(3):
                add("w_in_2", ("w_in_2", l, sec + g), [(name, l, g, j) for j in range(2)], 1024)
        for g in range(3):
            add("w_in_2", ("w_in_2v", l, 6 + g), [("dv", l, g, j) for j in range(2)], 1024)
        for q in range(8):
            add("w_in_2", ("w_in_2", l, 12 + q), [("gate", l, 2 * q + j) for j in range(2)], 1024)
        for name in ("w_proj_b_2", "w_proj_a_2"):
            add(name, (name, l), [(name, l, j) for j in range(2)], 1024)
        rows("w_out_2", l, KT)
        for f in range(FT // 2):
            for name, sec in (("up_a", 0), ("up_b", FT // 2)):
                add("w_up_2", ("w_up_2", l, sec + f), [(name, l, 2 * f + j) for j in range(2)], 1024)
        rows("w_down_2", l, FT)
    return chunks, number


def build(nc, t, out):
    F = mybir.dt.float32
    R = mybir.dt.float32r
    BF = mybir.dt.bfloat16
    I32 = mybir.dt.int32
    ALU = mybir.AluOpType
    ACT = mybir.ActivationFunctionType
    AX = mybir.AxisListType

    chunks, W = weight_plan()
    pieces, chunk_of = [], []
    for c, (_, _, ps) in enumerate(chunks):
        for j, (_, words) in enumerate(ps):
            pieces.append((c, j, words))
    last_piece = []
    for c, (_, _, ps) in enumerate(chunks):
        last_piece.append(W[ps[-1][0]])
    NP_ = len(pieces)

    W_BANK = {}
    POOL_BANK = (6, 7)
    STAT_BANK = 6
    STAGES = 3 + 2 * LAYERS
    SETUP = 11
    SBO = [0, 512, 896, 1152, 1280]
    TURN = (6.28125, 2029.0 / 2 ** 20, TWO_PI - 6.28125 - 2029.0 / 2 ** 20)
    ROUND = 1.5 * 2 ** 23

    def PAIR_KEYS(p):
        keys = [("w_in", sec + 2 * p + j) for sec in (CA, CB, CG, AV, AG) for j in range(2)]
        keys.append(("pool_w", p))
        return keys + [("w_in", sec + 2 * p + j) for sec in (BC, BH, BB, BG) for j in range(2)]

    def DIL_KEYS(l):
        return [(name, l, g, j) for name in ("dq", "dk", "dv") for g in range(3) for j in range(2)]

    count = 0
    for key in W:
        if key[0] in ("w_in", "w_branch"):
            W_BANK[key] = count % 6
            count += 1
        elif key[0] in ("sq", "sk", "dq", "dk", "gate"):
            W_BANK[key] = key[-1] % 2
        elif key[0] in ("sv", "dv"):
            W_BANK[key] = 0
        elif key[0] in ("up_a", "up_b"):
            W_BANK[key] = (2 * key[2] + (key[0] == "up_b") * 2 - key[2] % 2) % 8

    base = (nc.sbuf_base + 63) // 64 * 64
    top = nc.sbuf_usable_end
    at = [base]

    def keep(name, shape, dt=F):
        size = int(np.prod(shape[1:])) * (2 if dt == BF else 4)
        size = (size + 31) // 32 * 32
        h = nc.alloc_sbuf_tensor_at(name, shape, dt, offset=at[0])
        at[0] += size
        return h

    x = keep("x", [P, TB, D])
    hT = keep("hT", [P, 2, KT, SEQ], R)
    raw = keep("raw", [P, 2, 2048])
    whl = keep("whl", [P, 4, 2, 1024], R)
    cst = keep("cst", [P, NKEEP])
    onesd = keep("onesd", [P, P])
    negones = keep("negones", [P, P])
    identb = keep("identb", [P, P], BF)
    bandb = keep("bandb", [P, 516], BF)
    ownb = keep("ownb", [P, 256], BF)
    sbaddb = keep("sbaddb", [P, P], BF)
    vcol = keep("vcol", [P, NVEC])
    halfb = keep("halfb", [P, 96 + 32])
    stat = keep("stat", [P, 160])
    table = keep("table", [P, 2, SEQ])
    arena = at[0]

    def over(name, offset, shape, dt=F):
        size = int(np.prod(shape[1:])) * (2 if dt == BF else 4)
        assert arena + offset + size <= top, (name, arena + offset + size - top)
        return nc.alloc_sbuf_tensor_at(name, shape, dt, offset=arena + offset)

    K = 1024
    ada = over("ada", 0, [P, 8, 2048])
    vstage = over("vstage", 64 * K, [P, 6, P])
    cstage = over("cstage", 68 * K, [P, NCONST - NKEEP])
    crep = over("crep", 72 * K, [P, KT, P])
    badag = over("badag", 76 * K, [P, D])
    utmp = over("utmp", 80 * K, [P, SEQ])
    xn1 = over("xn1", 82 * K, [P, TB, D])
    yahl = over("yahl", 0, [P, 2, KT, SEQ], R)
    sag = over("sag", 16 * K, [P, KT, SEQ])
    ybf = over("ybf", 32 * K, [P, KT, SEQ])
    hc = over("hc", 48 * K, [P, KT, SEQ])
    cg = over("cg", 64 * K, [P, KT, SEQ])
    o = 80 * K
    glu = over("glu", o, [P, 2, SEQ + CF_TAPS - 1])
    acc1 = over("acc1", o + 4352, [P, SEQ])
    vpad = over("vpad", o + 6400, [P, 16 + SEQ])
    poolhl = over("poolhl", o + 8512, [P, 2, 2, SEQ], R)
    sbuf1 = over("sbuf1", o + 8512, [P, 2, 2 * SEQ])
    sbg = over("sbg", o + 8512, [P, 2, SEQ])
    yaf = over("yaf", o + 16704, [P, 16 + SEQ])
    mT = over("mT", o, [P, KT, SEQ])
    tg = over("tg", o + 16384, [P, SEQ])
    ybhi = over("ybhi", 0, [P, KT, SEQ], R)
    yblo = over("yblo", 32 * K, [P, KT, SEQ], R)
    sq = over("sq", 16 * K, [P, KT, SEQ])
    ychi = over("ychi", 16 * K, [P, KT, SEQ], R)
    yclo = over("yclo", 48 * K, [P, KT, SEQ], R)
    mhi = over("mhi", 64 * K, [P, KT, SEQ], R)
    mlo = over("mlo", 32 * K, [P, KT, SEQ], R)
    lnrow = over("lnrow", 0, [P, 2, D])
    prod = over("prod", 8 * K, [P, 2, SEQ])
    pos_i = over("pos_i", 12 * K, [P, SEQ], I32)
    ang = over("ang", 14 * K, [P, SEQ])
    rt = over("rt", 16 * K, [P, 3, SEQ])
    qd = over("qd", 0, [P, 3, 2, SEQ])
    kd = over("kd", 12 * K, [P, 3, 2, SEQ])
    vd = over("vd", 24 * K, [P, 3, TB, 256])
    sbq = over("sbq", 36 * K, [P, 2, SEQ])
    sbk = over("sbk", 40 * K, [P, 2, SEQ])
    sbv = over("sbv", 44 * K, [P, TB, 256])
    prob = over("prob", 36 * K, [P, 2, 768])
    probT = over("probT", 42 * K, [P, 2, 768])
    gates = over("gates", 48 * K, [P, 16, SEQ])
    sbl = over("sbl", 64 * K, [P, 1280])
    sbs = over("sbs", 69 * K, [P, 1280])
    sba = over("sba", 74 * K, [P, 1280])
    oaT = over("oaT", 80 * K, [P, 2, 2, SEQ], R)
    obT = over("obT", 88 * K, [P, 2, 2, SEQ], R)
    qraw = over("qraw", 80 * K, [P, 2, SEQ])
    rot = over("rot", 84 * K, [P, 2, SEQ])
    osb = over("osb", 96 * K, [P, 2, 256])
    ff = over("ff", 0, [P, FT, 2, SEQ], R)
    xn2 = over("xn2", 88 * K, [P, 2, D])
    apad = over("apad", 88 * K, [P, 2, SEQ + 2])
    facc = over("facc", 88 * K + 4128, [P, SEQ])
    fsil = over("fsil", 88 * K + 6176, [P, 2, SEQ])
    frow = over("frow", 0, [P, D])

    ident = cst[:, COFF["ident"]:COFF["ident"] + P]
    negtri = cst[:, COFF["negtri"]:COFF["negtri"] + P]
    swapm = cst[:, COFF["swap"]:COFF["swap"] + P]
    sbmul = cst[:, COFF["sbmul"]:COFF["sbmul"] + P]
    freq = cst[:, COFF["freq"]:COFF["freq"] + 1]
    sign = cst[:, COFF["sign"]:COFF["sign"] + 1]

    gaterow = table[:, :, :].rearrange("p a b -> p (a b)")

    def col(name, i):
        return vcol[:, VOFF[name] + i:VOFF[name] + i + 1]

    bnst, mv, ssq, msq, rstd, neghalf = stat[:, 0:48], stat[:, 48:56], stat[:, 56:60], stat[:, 60:64], stat[:, 64:68], stat[:, 68:72]
    modc, cact, nmax, den, rden = stat[:, 72:88], stat[:, 88:96], stat[:, 96:112], stat[:, 112:128], stat[:, 128:144]

    ctx = ExitStack()
    with ctx:
        psum = ctx.enter_context(nc.psum_tensor("psum", [P, 8 * SEQ], F))

        def bank(b):
            return psum[:, b * SEQ:(b + 1) * SEQ]

        def sem(name):
            return ctx.enter_context(nc.semaphore(name))

        raw_in = [sem("raw_in0"), sem("raw_in1")]
        w_hi, w_lo, w_used = sem("w_hi"), sem("w_lo"), sem("w_used")
        s_x, s_vec, s_cst, s_ada, s_adag, s_bcast = (sem(n) for n in ("x_in", "vec_in", "cst_in", "ada_in", "adag_in", "bcast_in"))
        s_vT, s_vcol, s_mod, s_modc, s_gp, s_gate = (sem(n) for n in ("vecT", "vcol_ready", "mod_psum", "modc_ready", "gate_psum", "gate_ready"))
        s_ini, s_cact, s_crep = sem("setup_done"), sem("cact_ready"), sem("crep_ready")
        s_ssq, s_ms, s_rstd, s_xn, s_xT, h_hi, h_lo = (sem(n) for n in ("sumsq", "ms_ready", "rstd_ready", "xn_ready", "xT_done", "h_hi", "h_lo"))
        x_ready = sem("x_ready")
        act_read, dve_read = sem("act_read"), sem("dve_read")
        pooled_f, pooled_hi, pooled_lo, ya_f, ya_hi, ya_lo, yb_f, hc_done = (sem(n) for n in ("pooled_f", "pooled_hi", "pooled_lo", "ya_f", "ya_hi", "ya_lo", "yb_f", "hc_done"))
        m_part, yb_hi, yb_lo, mean_ps, sqd, cen, var_ps, ve, sqr, rinv, nrm, ycs, ycf, yc_hi, yc_lo, m_hi, m_lo = (
            sem(n) for n in ("m_part", "yb_hi", "yb_lo", "mean_psum", "squared", "centred", "var_psum", "var_eps", "std_ready", "inv_std",
                             "normed", "yc_silu", "yc_f", "yc_hi", "yc_lo", "m_hi", "m_lo"))
        row_full, row_read, s_ln, s_rt, s_pos, s_tab = (sem(n) for n in ("row_full", "row_read", "lnrow_in", "rot_steps", "pos_in", "tables_ready"))
        q_raw, rot_ps, rope_done, z_ps, sb_abs, sb_l, sp_ready, e_ps, sb_attn, sbo_ps, ob_hi, ob_lo = (
            sem(n) for n in ("q_raw", "rot_psum", "rope_done", "z_psum", "sb_abs", "sb_log", "sp_ready", "e_psum", "sb_attn",
                             "sbo_psum", "ob_hi", "ob_lo"))
        s_ps, max_done, p_ready, pT_ps, pT_ready, o_ps, o_ready, oT_ps, oa_hi, oa_lo = (
            sem(n) for n in ("s_psum", "max_done", "p_ready", "pT_psum", "pT_ready", "o_psum", "o_ready", "oT_psum", "oa_hi", "oa_lo"))
        pb_ps, pb_f, pa_ps, pa_f, mix_f, mix_hi, mix_lo = (sem(n) for n in ("pb_psum", "pb_f", "pa_psum", "pa_f", "mix_f", "mix_hi", "mix_lo"))
        a_read, fconv, silu_done, b_read, ff_hi, ff_lo = (sem(n) for n in ("a_read", "ffn_conv", "silu_done", "b_read", "ff_hi", "ff_lo"))
        s_out, s_frow = sem("out_done"), sem("frow_in")
        dve_chain, act_chain, pool_chain = sem("dve_chain"), sem("act_chain"), sem("pool_chain")

        READER = {CA: "dve", CB: "act", CG: "act", AV: "act", AG: "act", BC: "act", BH: "dve", BB: "dve", BG: "act"}
        RSEM = {"act": act_read, "dve": dve_read}
        rcount = {}
        n = {"act": 0, "dve": 0}
        for key in W:
            who = None
            if key[0] == "w_in":
                sec = key[1] // 8 * 8
                who = READER.get(sec, "act")
            elif key[0] == "w_branch":
                who = "dve"
            elif key[0] in ("sq", "sk", "dq", "dk", "gate"):
                who = "act"
            elif key[0] in ("sv", "dv"):
                who = "act" if key[-1] == 1 else None
            elif key[0] == "up_a":
                who = "act"
            elif key[0] == "up_b":
                who = "dve"
            if who:
                n[who] += 1
                rcount[key] = (who, n[who])

        def read_of(key):
            who, v = rcount[key]
            return RSEM[who], v

        def await_read(eng, key):
            s, v = read_of(key)
            eng.wait_ge(s, v)

        def w_wait_full(eng, key):
            eng.wait_ge(w_used, W[key] + 1)

        def raw_view(w):
            c, j, words = pieces[w]
            tensor, key, ps = chunks[c]
            r = raw[:, c % 2, :]
            kind = ps[0][0][0]
            if kind == "pool_w":
                return r[:, 0:512].rearrange("p (a b) -> p a b", a=2)
            if kind in ("w_proj_a_2", "w_proj_b_2"):
                return r.rearrange("p (a b) -> p a b", a=2)[:, :, j * 512:(j + 1) * 512]
            if kind in ("w_out", "w_out_2", "w_down_2"):
                return r[:, j * 1024:(j + 1) * 1024].rearrange("p (a b) -> p a b", a=2)
            if kind in ("sv", "dv"):
                return r[:, j * 1024:(j + 1) * 1024].rearrange("p (a b) -> p a b", a=4)
            return r.rearrange("p (a b) -> p a b", a=8)[:, :, j * P:(j + 1) * P]

        def whl_view(w, part):
            a = raw_view(w).shape[1]
            n_ = pieces[w][2]
            return whl[:, w % 4, part, 0:n_].rearrange("p (a b) -> p a b", a=a)

        def split_hi(w):
            if w >= NP_:
                return
            c = pieces[w][0]
            nc.scalar.wait_ge(raw_in[c % 2], 16 * (c // 2 + 1))
            if w >= 4:
                nc.scalar.wait_ge(w_used, w - 3)
            nc.scalar.activation(whl_view(w, 0), raw_view(w), ACT.Copy).then_inc(w_hi, 1)

        def split_lo(w):
            if w >= NP_:
                return
            nc.vector.wait_ge(w_hi, w + 1)
            nc.vector.tensor_tensor(whl_view(w, 1), raw_view(w), whl_view(w, 0).bitcast(F),
                                    ALU.subtract).then_inc(w_lo, 1)

        ROWS = [("w_out", None, KT)] + [s for l in range(LAYERS) for s in (("w_out_2", l, KT), ("w_down_2", l, FT))]

        def row_index(stage, half, tb):
            return ROWS.index(stage) * 8 + half * 4 + tb

        def row_wait(eng, stage, half, tb):
            name, l, nk = stage
            if tb < 3:
                eng.wait_ge(row_full, ROWS.index(stage) * 6 + half * 3 + tb + 1)
            else:
                eng.wait_ge(w_used, W[(name, l, half, nk - 2)] + 1)

        def row_reads(stage, half, tb):
            i = ROWS.index(stage)
            return 4 * half + tb + 1 if i == 0 else 8 + 4 * (i - 1) + tb + 1

        def proj_wait(eng, s_full, name, l, j, mm):
            if mm < 3:
                eng.wait_ge(s_full, 6 * l + 3 * j + mm + 1)
            else:
                eng.wait_ge(w_used, W[(name, l, j)] + 1)

        NVEC_DMA = 0
        for name, rows in VECS:
            done = 0
            while done < rows:
                g = VOFF[name] + done
                done += min(rows - done, P - g % P)
                NVEC_DMA += 1

        block = ctx.enter_context(nc.Block())

        def chunk_src(c):
            tensor, key, ps = chunks[c]
            kind = key[0]
            a = t[tensor]
            if kind == "w_in":
                c0 = (key[1] + 2 * key[2]) * P
                return a[0].rearrange("(k p) n -> p k n", p=P)[:, :, c0:c0 + 256], (8, 256)
            if kind == "pool_w":
                return a[0, key[1]].rearrange("(k p) n -> p k n", p=P), (2, 256)
            if kind == "w_branch":
                return a[0, key[1]].rearrange("(k p) n -> p k n", p=P)[:, :, key[2] * 256:key[2] * 256 + 256], (8, 256)
            if kind in ("w_out", "w_out_2", "w_down_2"):
                _, l, half, k0, nk = key
                return a[l or 0].rearrange("(k p) n -> p k n", p=P)[:, k0:k0 + nk, half * 512:half * 512 + 512], (nk, 512)
            if kind in ("w_in_2", "w_in_2v", "w_up_2"):
                _, l, sec = key
                return a[l].rearrange("(k p) n -> p k n", p=P)[:, :, sec * 256:sec * 256 + 256], (8, 256)
            return a[key[1]].rearrange("(k p) n -> p k n", p=P), (2, 1024)

        @block.sync
        def _(sp):
            xr = t["x"][0].rearrange("(b p) d -> p b d", p=P)
            for tb in range(TB):
                sp.dma_start(x[:, tb, :], xr[:, tb, :]).then_inc(s_x, 16)
            wa = t["w_ada"][0].rearrange("(k p) n -> p k n", p=P)
            for q in range(8):
                sp.dma_start(ada[:, q, :].rearrange("p (k n) -> p k n", k=KT), wa[:, :, q * 256:(q + 1) * 256]).then_inc(s_ada, 16)

            def chunk_load(c):
                src, (a, b) = chunk_src(c)
                if c >= 2:
                    sp.wait_ge(w_lo, last_piece[c - 2] + 1)
                sp.dma_start(raw[:, c % 2, 0:a * b].rearrange("p (a b) -> p a b", a=a), src).then_inc(raw_in[c % 2], 16)

            chunk_load(0)
            chunk_load(1)
            sp.wait_ge(s_mod, 1)
            for q in range(4):
                sp.dma_start(ada[:, q, :].rearrange("p (k n) -> p k n", k=KT), wa[:, :, 2048 + q * 256:2048 + (q + 1) * 256]).then_inc(s_adag, 16)
            for c in range(2, len(chunks)):
                if chunks[c][0] == "w_out" and chunks[c - 1][0] != "w_out":
                    w_wait_full(sp, ("w_branch", 1, 7))
                    sp.dma_start(lnrow[:, 0, :], t["ln_g"].to_broadcast((P, D))).then_inc(s_ln, 16)
                    sp.dma_start(lnrow[:, 1, :], t["ln_b"].to_broadcast((P, D))).then_inc(s_ln, 16)
                    sp.dma_start(pos_i[:], t["positions_2"].to_broadcast((P, SEQ))).then_inc(s_pos, 16)
                chunk_load(c)
            w_wait_full(sp, ("w_down_2", LAYERS - 1, 1, FT - 2))
            sp.dma_start(frow[:], t["norm_final_2"].rearrange("(a n) -> a n", a=1).to_broadcast((P, D))).then_inc(s_frow, 16)
            ov = out[0].rearrange("(b p) d -> p b d", p=P)
            for tb in range(TB):
                sp.wait_ge(s_xn, 4 * (STAGES - 1) + tb + 1)
                sp.dma_start(ov[:, tb, :], x[:, tb, :]).then_inc(s_out, 16)
            sp.wait_ge(s_out, 16 * TB)

        @block.gpsimd
        def _(pool):
            for name, rows in VECS:
                src = t[{"norm_mix": "norm_mix_2", "b_gate": "b_gate_2", "norm_ffn": "norm_ffn_2",
                         "conv_w": "conv_w_2", "conv_b": "conv_b_2"}.get(name, name)]
                dims = " ".join("abc"[:len(src.shape)])
                src = src.rearrange(f"{dims} -> ({dims})").rearrange("(r n) -> r n", n=P)
                done = 0
                while done < rows:
                    g = VOFF[name] + done
                    m = min(rows - done, P - g % P)
                    pool.dma_start(vstage[g % P:g % P + m, g // P, :], src[done:done + m, :]).then_inc(s_vec, 16)
                    done += m
            nc.gpsimd.memset(neghalf, -0.5).then_inc(pool_chain, 1)
            pool.wait_ge(pool_chain, 1)
            for s in range(STAGES):
                for tb in range(TB):
                    pool.wait_ge(s_ms, 4 * s + tb + 1)
                    if s:
                        pool.wait_ge(s_xn, 4 * (s - 1) + tb + 1)
                    nc.gpsimd.tensor_tensor(rstd[:, tb:tb + 1], msq[:, tb:tb + 1], neghalf[:, 0:1], ALU.pow).then_inc(s_rstd, 1)

        @block.scalar
        def _(act):
            chain = [0]

            def link(ins):
                chain[0] += 1
                ins.then_inc(act_chain, 1)
                act.wait_ge(act_chain, chain[0])

            A = nc.scalar.activation
            act.dma_start(cst[:], t["consts"][:, 0:NKEEP]).then_inc(s_cst, 16)
            act.dma_start(cstage[:], t["consts"][:, NKEEP:NCONST]).then_inc(s_cst, 16)
            act.dma_start(badag[:], t["b_ada"][:, 2048:3072].to_broadcast((P, D))).then_inc(s_bcast, 16)
            act.wait_ge(s_vcol, 1)
            A(cact, vcol[:, VOFF["c"]:VOFF["c"] + 8], ACT.Silu).then_inc(s_cact, 1)
            for w in range(3):
                split_hi(w)
            act.wait_ge(s_modc, 1)
            act.wait_ge(s_xT, 4)
            for ct in range(KT):
                A(hT[:, 0, ct, :], bank(ct), ACT.Identity, bias=modc[:, ct:ct + 1], scale=modc[:, 8 + ct:9 + ct]).then_inc(h_hi, 1)

            def pair_step(p, key, j):
                tt = 2 * p + j
                sec = key[1] // 8 * 8 if key[0] == "w_in" else None
                b = W_BANK[key]
                bias = col("b_in", key[1]) if sec is not None else None
                if sec in (CB, CG, AV, AG, BC, BG):
                    w_wait_full(act, key)
                if sec == CB:
                    if p:
                        act.wait_ge(hc_done, tt - 1)
                    A(glu[:, j, CF_TAPS - 1:], bank(b), ACT.Tanh, bias=halfb[:, key[1]:key[1] + 1], scale=0.5).then_inc(act_read, 1)
                elif sec == CG:
                    A(cg[:, tt, :], bank(b), ACT.Silu, bias=bias).then_inc(act_read, 1)
                elif sec == AV:
                    if tt:
                        act.wait_ge(pooled_lo, tt)
                    A(vpad[:, 16:], bank(b), ACT.Identity, bias=bias).then_inc(act_read, 1)
                elif sec == AG:
                    A(sag[:, tt, :], bank(b), ACT.Silu, bias=bias).then_inc(act_read, 1)
                elif sec == BC:
                    A(ybf[:, tt, :], bank(b), ACT.Identity, bias=bias).then_inc(act_read, 1)
                elif sec == BG:
                    A(sbg[:, j, :], bank(b), ACT.Silu, bias=bias).then_inc(act_read, 1)

            def pooled_split(tt):
                act.wait_ge(pooled_f, tt + 1)
                if tt >= 2:
                    w_wait_full(act, ("pool_w", tt // 2 - 1))
                A(poolhl[:, tt % 2, 0, :], vpad[:, 16:], ACT.Copy).then_inc(pooled_hi, 1)

            act.wait_ge(s_ini, SETUP)
            for p in range(4):
                for key in PAIR_KEYS(p):
                    w = W[key]
                    split_hi(w + 3)
                    j = key[1] % 2
                    if key[0] == "pool_w":
                        for jj in range(2):
                            tt = 2 * p + jj
                            act.wait_ge(ya_f, tt + 1)
                            A(yahl[:, 0, tt, :], yaf[:, 0:SEQ], ACT.Copy).then_inc(ya_hi, 1)
                        continue
                    pair_step(p, key, j)
                    if key[0] == "w_in" and key[1] // 8 * 8 == AV:
                        pooled_split(2 * p + j)

            def mixture_hi(m):
                act.wait_ge(m_part, 8 + m + 1)
                A(mhi[:, m, :], mT[:, m, :], ACT.Copy).then_inc(m_hi, 1)

            for i in range(3):
                for q in range(4):
                    for j in range(2):
                        m = 2 * q + j
                        key = ("w_in", MG + 8 * i + m)
                        split_hi(W[key] + 3)
                        if i == 0 and m == 0:
                            act.wait_ge(hc_done, KT)
                            act.wait_ge(ya_lo, KT)
                        if i == 1 and m == 0:
                            w_wait_full(act, ("w_branch", 0, 7))
                            for k in range(KT):
                                A(ybhi[:, k, :], ybf[:, k, :], ACT.Copy).then_inc(yb_hi, 1)
                        if i == 1 and m == 3:
                            for k in range(KT):
                                act.wait_ge(cen, k + 1)
                                A(sq[:, k, :], hc[:, k, :], ACT.Square).then_inc(sqd, 1)
                        if i == 1 and m == 5:
                            act.wait_ge(ve, 1)
                            A(sq[:, 0, :], sq[:, 0, :], ACT.Sqrt).then_inc(sqr, 1)
                        if i == 1 and m == 6:
                            for k in range(KT):
                                act.wait_ge(nrm, k + 1)
                                A(hc[:, k, :], hc[:, k, :], ACT.Silu, bias=col("cf_ln_b", k), scale=col("cf_ln_g", k)).then_inc(ycs, 1)
                        if i == 1 and m == 7:
                            for k in range(KT):
                                act.wait_ge(ycf, k + 1)
                                A(ychi[:, k, :], hc[:, k, :], ACT.Copy).then_inc(yc_hi, 1)
                    for j in range(2):
                        m = 2 * q + j
                        key = ("w_in", MG + 8 * i + m)
                        split_hi(W[("w_branch", i, m)] + 3)
                        w_wait_full(act, key)
                        if i and 8 * (i - 1) + m:
                            act.wait_ge(m_part, 8 * (i - 1) + m)
                        A(mT[:, m, :] if i == 0 else tg[:], bank(W_BANK[key]), ACT.Tanh, bias=halfb[:, key[1]:key[1] + 1],
                          scale=0.5).then_inc(act_read, 1)
                        if i == 2 and m:
                            mixture_hi(m - 1)
            mixture_hi(KT - 1)

            def lead(keys):
                for key in keys:
                    split_hi(W[key] + 3)

            lead([("w_out", None, half, k) for half in range(2) for k in range(0, KT, 2)])
            act.wait_ge(s_rt, 1)
            act.wait_ge(row_read, 4)
            A(table[:, 0, :], rt[:, 0, :], ACT.Sin).then_inc(s_tab, 1)
            act.wait_ge(s_rt, 2)
            A(rt[:, 1, :], rt[:, 1, :], ACT.Sin).then_inc(s_tab, 1)

            def norm_sums(s):
                for tb in range(TB):
                    act.wait_ge(x_ready, 4 * (s - 2) + tb + 1)
                    if tb >= 2 and s < STAGES - 1:
                        act.wait_ge(s_xT, 4 * (s - 1) + tb - 1)
                    elif tb >= 2:
                        act.wait_ge(s_ssq, 4 * (s - 2) + tb - 1)
                    A(xn2[:, tb % 2, :], x[:, tb, :], ACT.Square, accum_out=ssq[:, tb:tb + 1]).then_inc(s_ssq, 1)

            def norm_hi(s, name, l):
                act.wait_ge(s_xT, 4 * s)
                for ct in range(KT):
                    A(hT[:, 0, ct, :], bank(ct), ACT.Identity, scale=col(name, 8 * l + ct)).then_inc(h_hi, 1)

            for l in range(LAYERS):
                s = 2 + 2 * l
                norm_sums(s)
                norm_hi(s, "norm_mix", l)
                nc.scalar.preload_act_table_set("natural_log_exp_and_others")
                for name, dst, sc in (("sq", sbq, HEAD ** -0.5), ("sk", sbk, 1.0)):
                    for j in range(2):
                        key = (name, l, j)
                        split_hi(W[key] + 3)
                        w_wait_full(act, key)
                        A(dst[:, j, :], bank(W_BANK[key]), ACT.Copy, scale=sc).then_inc(act_read, 1)
                for j in range(2):
                    key = ("sv", l, j)
                    split_hi(W[key] + 3)
                w_wait_full(act, key)
                b = W_BANK[key]
                A(sbv[:].rearrange("p a b -> p (a b)"), psum[:, b * SEQ:(b + 2) * SEQ], ACT.Copy).then_inc(act_read, 1)

                def sb_logs(h):
                    for kb in range(TB):
                        act.wait_ge(z_ps, 4 * (4 * l + h) + kb + 1)
                        A(sbl[:, SBO[kb]:SBO[kb + 1]], bank(2 + kb)[:, 0:SBO[kb + 1] - SBO[kb]], ACT.Abs).then_inc(sb_abs, 1)
                    for kb in range(TB):
                        act.wait_ge(sb_abs, 4 * (4 * l + h) + kb + 1)
                        v = sbl[:, SBO[kb]:SBO[kb + 1]]
                        A(v, v, ACT.Exp, scale=-1.0).then_inc(act_chain, 1)
                    chain[0] += 4
                    for kb in range(TB):
                        act.wait_ge(act_chain, chain[0] - 3 + kb)
                        v = sbl[:, SBO[kb]:SBO[kb + 1]]
                        A(v, v, ACT.Ln, bias=1.0).then_inc(sb_l, 1)

                def sb_exp(h):
                    for kb in range(TB):
                        act.wait_ge(e_ps, 4 * (4 * l + h) + kb + 1)
                        if kb == 0 and h:
                            act.wait_ge(sbo_ps, 4 * l + h)
                        A(sba[:, SBO[kb]:SBO[kb + 1]], bank(2 + kb)[:, 0:SBO[kb + 1] - SBO[kb]], ACT.Exp).then_inc(sb_attn, 1)

                def sb_out(h):
                    act.wait_ge(sbo_ps, 4 * l + h + 1)
                    po = h % 2 * HEAD
                    A(obT[po:po + HEAD, h // 2, 0, :], bank(6)[po:po + HEAD, :], ACT.Copy).then_inc(ob_hi, 1)

                for n_, key in enumerate(DIL_KEYS(l)):
                    split_hi(W[key] + 3)
                    if key[0] in ("dq", "dk"):
                        w_wait_full(act, key)
                        if n_ >= 2:
                            act.wait_ge(rope_done, 12 * l + n_ - 1)
                        A(qraw[:, n_ % 2, :], bank(W_BANK[key]), ACT.Copy,
                          scale=HEAD ** -0.5 if key[0] == "dq" else 1.0).then_inc(act_read, 1)
                    elif key[3] == 1:
                        w_wait_full(act, key)
                        b = W_BANK[key]
                        A(vd[:, key[2], :, :].rearrange("p a b -> p (a b)"), psum[:, b * SEQ:(b + 2) * SEQ], ACT.Copy).then_inc(act_read, 1)
                    h, ph = n_ // 4, n_ % 4
                    if ph == 0 and h >= 1:
                        sb_out(h - 1)
                    if ph == 0 and h < 4:
                        sb_logs(h)
                    if ph == 2 and h < 4:
                        sb_exp(h)

                def dil_exp(u):
                    act.wait_ge(max_done, 16 * l + u + 1)
                    if u >= 2:
                        act.wait_ge(pT_ps, 16 * l + u - 1)
                    A(prob[:, u % 2, :], psum[:, 2 * SEQ:2 * SEQ + 768], ACT.Exp, bias=nmax[:, u:u + 1],
                      accum_out=den[:, u:u + 1]).then_inc(p_ready, 1)

                def dil_pT(u):
                    act.wait_ge(pT_ps, 16 * l + u + 1)
                    if u >= 2:
                        act.wait_ge(o_ps, 16 * l + u - 1)
                    A(probT[:, u % 2, :], psum[:, 4 * SEQ:4 * SEQ + 768], ACT.Copy).then_inc(pT_ready, 1)

                def dil_oT(r):
                    act.wait_ge(oT_ps, 4 * l + r + 1)
                    A(oaT[:, :, 0, r:SEQ:4], bank(7)[:, 0:256].rearrange("p (a b) -> p a b", a=2), ACT.Copy).then_inc(oa_hi, 1)

                for u in range(16):
                    key = ("gate", l, u)
                    split_hi(W[key] + 3)
                    dil_exp(u)
                    w_wait_full(act, key)
                    A(gates[:, u, :], bank(W_BANK[key]), ACT.Tanh, bias=halfb[:, 96 + 16 * l + u:97 + 16 * l + u], scale=0.5).then_inc(act_read, 1)
                    dil_pT(u)
                    if u % 4 == 3 and u > 4:
                        dil_oT(u // 4 - 1)
                lead([("w_proj_b_2", l, 0), ("w_proj_b_2", l, 1)])
                dil_oT(3)
                lead([("w_proj_a_2", l, 0)])
                for m in range(KT):
                    if m == 4:
                        lead([("w_proj_a_2", l, 1)])
                    act.wait_ge(mix_f, 8 * l + m + 1)
                    A(hT[:, 0, m, :], gates[:, m, :], ACT.Copy).then_inc(mix_hi, 1)
                lead([("w_out_2", l, half, k) for half in range(2) for k in range(0, KT, 2)])
                norm_sums(s + 1)
                norm_hi(s + 1, "norm_ffn", l)
                for f2 in range(FT // 2):
                    for j in range(2):
                        f = 2 * f2 + j
                        key = ("up_a", l, f)
                        split_hi(W[key] + 3)
                        w_wait_full(act, key)
                        if FT * l + f >= 2:
                            act.wait_ge(fconv, FT * l + f - 1)
                        A(apad[:, j, 2:], bank(W_BANK[key]), ACT.Copy).then_inc(act_read, 1)
                    for j in range(2):
                        f = 2 * f2 + j
                        act.wait_ge(fconv, FT * l + f + 1)
                        if FT * l + f >= 2:
                            act.wait_ge(ff_lo, FT * l + f - 1)
                        A(fsil[:, j, :], facc[:], ACT.Silu).then_inc(silu_done, 1)
                    for j in range(2):
                        f = 2 * f2 + j
                        key = ("up_b", l, f)
                        split_hi(W[key] + 3)
                        await_read(act, key)
                        A(ff[:, f, 0, :], fsil[:, j, :], ACT.Copy).then_inc(ff_hi, 1)
                lead([("w_down_2", l, half, k) for half in range(2) for k in range(0, FT, 2)])
            norm_sums(2 + 2 * LAYERS)

        @block.vector
        def _(dve):
            V = nc.vector
            chain = [0]

            def link(ins):
                chain[0] += 1
                ins.then_inc(dve_chain, 1)
                dve.wait_ge(dve_chain, chain[0])

            def step(ins):
                chain[0] += 1
                ins.then_inc(dve_chain, 1)
                return chain[0]

            V.memset(onesd[:], 1.0 / D).then_inc(s_ini, 1)
            V.memset(negones[:], -1.0).then_inc(s_ini, 1)
            dve.wait_ge(s_cst, 32)
            V.tensor_copy(identb[:], ident).then_inc(s_ini, 1)
            c0 = COFF["band"]
            V.tensor_copy(bandb[:], cstage[:, 0:516]).then_inc(s_ini, 1)
            V.tensor_copy(ownb[:], cstage[:, COFF["own"] - c0:COFF["own"] - c0 + 256]).then_inc(s_ini, 1)
            V.tensor_copy(sbaddb[:], cstage[:, COFF["sbadd"] - c0:COFF["sbadd"] - c0 + P]).then_inc(s_ini, 1)
            dve.wait_ge(s_vT, 6)
            V.tensor_copy(vcol[:, 0:512], bank(0)).then_inc(s_ini, 1)
            V.tensor_copy(vcol[:, 512:NVEC], bank(1)[:, 0:NVEC - 512]).then_inc(s_vcol, 1)
            dve.wait_ge(s_ini, 7)
            dve.wait_ge(s_vcol, 1)
            V.tensor_scalar(halfb[:, 0:96], vcol[:, 0:96], 0.5, None, ALU.mult).then_inc(s_ini, 1)
            V.tensor_scalar(halfb[:, 96:128], vcol[:, VOFF["b_gate"]:VOFF["b_gate"] + 32], 0.5, None, ALU.mult).then_inc(s_ini, 1)

            def layer_norm_rows(s):
                for tb in range(TB):
                    for half in range(2):
                        ins = V.bn_stats(bnst[:, (2 * tb + half) * 6:(2 * tb + half) * 6 + 6], x[:, tb, half * 512:(half + 1) * 512])
                        k_ = step(ins)
                    dve.wait_ge(dve_chain, k_)
                    link(V.bn_aggr(mv[:, 2 * tb:2 * tb + 2], bnst[:, 12 * tb:12 * tb + 12].rearrange("p (a b) -> p a b", a=2)))
                    V.tensor_scalar(msq[:, tb:tb + 1], mv[:, 2 * tb + 1:2 * tb + 2], LN_EPS, None, ALU.add).then_inc(s_ms, 1)

            dve.wait_ge(s_x, 16 * TB)
            layer_norm_rows(0)
            for tb in range(TB):
                dve.wait_ge(s_rstd, tb + 1)
                V.tensor_scalar(xn1[:, tb, :], x[:, tb, :], mv[:, 2 * tb:2 * tb + 1], rstd[:, tb:tb + 1],
                                ALU.subtract, ALU.mult).then_inc(s_xn, 1)
            dve.wait_ge(s_cact, 1)
            for k in range(KT):
                V.tensor_copy(crep[:, k, :], cact[:, k:k + 1].to_broadcast((P, P))).then_inc(s_crep, 1)
            dve.wait_ge(s_mod, 1)
            link(V.tensor_tensor(modc, bank(7)[:, 0:16], vcol[:, VOFF["b_ada"]:VOFF["b_ada"] + 16], ALU.add))
            V.tensor_scalar(modc[:, 8:16], modc[:, 8:16], 1.0, None, ALU.add).then_inc(s_modc, 1)
            for w in range(3):
                split_lo(w)
            dve.wait_ge(s_xT, 4)
            dve.wait_ge(s_modc, 1)
            for ct in range(KT):
                dve.wait_ge(h_hi, ct + 1)
                if ct:
                    dve.wait_ge(h_lo, ct)
                link(V.tensor_scalar(utmp[:], bank(ct), modc[:, 8 + ct:9 + ct], modc[:, ct:ct + 1], ALU.mult, ALU.add))
                V.tensor_tensor(hT[:, 1, ct, :], utmp[:], hT[:, 0, ct, :].bitcast(F), ALU.subtract).then_inc(h_lo, 1)
            dve.wait_ge(h_lo, KT)
            V.memset(glu[:, :, 0:CF_TAPS - 1], 0.0).then_inc(s_ini, 1)
            V.memset(vpad[:, 0:16], 0.0).then_inc(s_ini, 1)

            conv = []

            def conv_start(tt):
                g = glu[:, tt % 2, :]
                steps = []

                def first(dst, k, bias):
                    def go():
                        if dst is acc1 and tt:
                            dve.wait_ge(hc_done, tt)
                        if bias is not None:
                            last[dst is acc1] = step(V.tensor_scalar(A_(dst), g[:, k:k + SEQ], col("cf_w", 8 * k + tt), bias, ALU.mult, ALU.add))
                        else:
                            last[dst is acc1] = step(V.tensor_scalar(A_(dst), g[:, k:k + SEQ], col("cf_w", 8 * k + tt), None, ALU.mult))
                    return go

                def A_(dst):
                    return acc1[:] if dst is acc1 else hc[:, tt, :]

                last = {False: 0, True: 0}

                def tap(dst, k):
                    def go():
                        dve.wait_ge(dve_chain, last[dst is acc1])
                        last[dst is acc1] = step(V.scalar_tensor_tensor(A_(dst), g[:, k:k + SEQ], col("cf_w", 8 * k + tt), A_(dst), ALU.mult, ALU.add))
                    return go

                def finish():
                    dve.wait_ge(dve_chain, max(last.values()))
                    V.tensor_tensor(hc[:, tt, :], hc[:, tt, :], acc1[:], ALU.add).then_inc(hc_done, 1)

                steps.append(first(hc, 0, col("cf_b", tt)))
                steps.append(first(acc1, 1, None))
                for k in range(2, CF_TAPS):
                    steps.append(tap(acc1 if k % 2 else hc, k))
                steps.append(finish)
                conv.extend(steps)

            def conv_run(n_):
                for _ in range(min(n_, len(conv))):
                    conv.pop(0)()

            def pair_step(p, key, j):
                tt = 2 * p + j
                if key[0] == "pool_w":
                    for jj in range(2):
                        tt = 2 * p + jj
                        w_wait_full(dve, key)
                        if jj == 0:
                            await_read(dve, ("w_in", AG + 2 * p + 1))
                        if tt:
                            dve.wait_ge(ya_lo, tt)
                        V.scalar_tensor_tensor(yaf[:, 0:SEQ], bank(POOL_BANK[tt % 2]), col("pool_scale", tt), sag[:, tt, :],
                                               ALU.mult, ALU.mult).then_inc(ya_f, 1)
                        dve.wait_ge(ya_hi, tt + 1)
                        V.tensor_tensor(yahl[:, 1, tt, :], yaf[:, 0:SEQ], yahl[:, 0, tt, :].bitcast(F), ALU.subtract).then_inc(ya_lo, 1)
                    return
                sec = key[1] // 8 * 8
                if sec == CB:
                    await_read(dve, key)
                    w_wait_full(dve, ("w_in", CA + tt))
                    gl = glu[:, j, CF_TAPS - 1:]
                    link(V.tensor_scalar(gl, gl, 0.5, 0.5, ALU.mult, ALU.add))
                    k_ = W_BANK[("w_in", CA + tt)]
                    V.scalar_tensor_tensor(gl, bank(k_), col("b_in", CA + tt), gl, ALU.add, ALU.mult).then_inc(dve_read, 1)
                    await_read(dve, ("w_in", CA + tt))
                    conv_start(tt)
                elif sec == AV:
                    await_read(dve, key)
                    if p:
                        w_wait_full(dve, ("pool_w", p - 1))
                    src, w_ = vpad, 1
                    for n_ in range(p + 1):
                        dst = sbuf1[:, j, :] if n_ % 2 == 0 else yaf[:]
                        lo_ = 2 ** (n_ + 1)
                        s_ = src[:] if src is vpad else src
                        link(V.tensor_tensor(dst[:, lo_:16 + SEQ], s_[:, lo_:16 + SEQ], s_[:, lo_ - w_:16 + SEQ - w_], ALU.add))
                        src, w_ = dst, w_ * 2
                    link(V.tensor_tensor(src[:, 16:32], src[:, 16:32], cst[:, COFF["corr"] + 16 * p:COFF["corr"] + 16 * p + 16], ALU.mult))
                    V.scalar_tensor_tensor(vpad[:, 16:], src[:, 16:16 + SEQ], 1.0 / w_, vpad[:, 16:], ALU.mult, ALU.subtract).then_inc(pooled_f, 1)
                    dve.wait_ge(pooled_hi, tt + 1)
                    V.tensor_tensor(poolhl[:, j, 1, :], vpad[:, 16:], poolhl[:, j, 0, :].bitcast(F), ALU.subtract).then_inc(pooled_lo, 1)
                elif sec == BH:
                    if j == 0:
                        link(V.memset(yaf[:, 0:2], 0.0))
                    w_wait_full(dve, key)
                    await_read(dve, ("w_in", BC + tt))
                    V.scalar_tensor_tensor(yaf[:, 2:2 + SEQ], bank(W_BANK[key]), col("b_in", key[1]), ybf[:, tt, :],
                                           ALU.add, ALU.mult).then_inc(dve_read, 1)
                    await_read(dve, key)
                    y = ybf[:, tt, :]
                    link(V.tensor_scalar(y, yaf[:, 2:2 + SEQ], col("sc_w", 16 + tt), col("sc_b", tt), ALU.mult, ALU.add))
                    link(V.scalar_tensor_tensor(y, yaf[:, 1:1 + SEQ], col("sc_w", 8 + tt), y, ALU.mult, ALU.add))
                    step(V.scalar_tensor_tensor(y, yaf[:, 0:SEQ], col("sc_w", tt), y, ALU.mult, ALU.add))
                    b_conv[tt] = chain[0]
                elif sec == BB:
                    w_wait_full(dve, key)
                    dve.wait_ge(dve_chain, b_conv[tt])
                    y = ybf[:, tt, :]
                    V.scalar_tensor_tensor(y, bank(W_BANK[key]), col("b_in", key[1]), y, ALU.add, ALU.mult).then_inc(dve_read, 1)
                elif sec == BG:
                    await_read(dve, key)
                    await_read(dve, ("w_in", BB + tt))
                    y = ybf[:, tt, :]
                    V.tensor_tensor(y, y, sbg[:, j, :], ALU.mult).then_inc(yb_f, 1)

            b_conv = {}
            dve.wait_ge(s_ini, SETUP)
            for p in range(4):
                for key in PAIR_KEYS(p):
                    split_lo(W[key] + 3)
                    pair_step(p, key, key[1] % 2)
                    if key == ("w_in", CG):
                        dve.wait_ge(s_gp, 1)
                        dve.wait_ge(s_bcast, 16)
                        link(V.tensor_tensor(gaterow, psum[:, 6 * SEQ:8 * SEQ], badag[:], ALU.add))
                        V.tensor_scalar(gaterow, gaterow, 0.5, None, ALU.mult).then_inc(s_gate, 1)
                    conv_run(5)

            def mixture_lo(m):
                dve.wait_ge(m_hi, m + 1)
                V.tensor_tensor(mlo[:, m, :], mT[:, m, :], mhi[:, m, :].bitcast(F), ALU.subtract).then_inc(m_lo, 1)

            def yb_split(k):
                dve.wait_ge(yb_hi, k + 1)
                V.tensor_tensor(yblo[:, k, :], ybf[:, k, :], ybhi[:, k, :].bitcast(F), ALU.subtract).then_inc(yb_lo, 1)

            for i in range(3):
                for q in range(4):
                    for j in range(2):
                        m = 2 * q + j
                        split_lo(W[("w_in", MG + 8 * i + m)] + 3)
                        if i == 0:
                            conv_run(6)
                        if i == 1 and m == 0:
                            for k in range(KT):
                                yb_split(k)
                        if i == 1 and m == 3:
                            dve.wait_ge(mean_ps, 1)
                            for k in range(KT):
                                V.tensor_tensor(hc[:, k, :], hc[:, k, :], bank(STAT_BANK), ALU.subtract).then_inc(cen, 1)
                        if i == 1 and m == 5:
                            dve.wait_ge(var_ps, 1)
                            V.tensor_scalar(sq[:, 0, :], bank(STAT_BANK), LN_EPS, None, ALU.add).then_inc(ve, 1)
                            dve.wait_ge(sqr, 1)
                            link(V.reciprocal(sq[:, 0, :], sq[:, 0, :]))
                            dve.wait_ge(cen, KT)
                            for k in range(KT):
                                V.tensor_tensor(hc[:, k, :], hc[:, k, :], sq[:, 0, :], ALU.mult).then_inc(nrm, 1)
                        if i == 1 and m == 7:
                            for k in range(KT):
                                dve.wait_ge(ycs, k + 1)
                                V.tensor_tensor(hc[:, k, :], hc[:, k, :], cg[:, k, :], ALU.mult).then_inc(ycf, 1)
                            for k in range(KT):
                                dve.wait_ge(yc_hi, k + 1)
                                V.tensor_tensor(yclo[:, k, :], hc[:, k, :], ychi[:, k, :].bitcast(F), ALU.subtract).then_inc(yc_lo, 1)
                    for j in range(2):
                        m = 2 * q + j
                        key = ("w_branch", i, m)
                        split_lo(W[key] + 3)
                        w_wait_full(dve, key)
                        await_read(dve, ("w_in", MG + 8 * i + m))
                        if i == 0:
                            V.scalar_tensor_tensor(mT[:, m, :], mT[:, m, :], 1.0, bank(W_BANK[key]), ALU.add, ALU.mult).then_inc(dve_read, 1)
                            conv_run(6)
                            continue
                        g = tg[:]
                        V.scalar_tensor_tensor(g, g, 1.0, bank(W_BANK[key]), ALU.add, ALU.mult).then_inc(dve_read, 1)
                        await_read(dve, key)
                        if i == 2:
                            dve.wait_ge(m_part, m + 1)
                        V.tensor_tensor(mT[:, m, :], mT[:, m, :], g, ALU.add).then_inc(m_part, 1)
                        if i == 2 and m:
                            mixture_lo(m - 1)
                if i == 0:
                    conv_run(len(conv))
            mixture_lo(KT - 1)

            w_wait_full(dve, ("w_branch", 2, 7))
            dve.wait_ge(s_pos, 16)
            link(V.tensor_copy(ang[:], pos_i[:]))
            link(V.tensor_scalar(ang[:], ang[:], freq, None, ALU.mult))
            for n_, quarter in ((0, 0.25), (1, 0.0)):
                turns, arg = rt[:, 2, :], rt[:, n_, :]
                link(V.tensor_scalar(turns, ang[:], 1.0 / TWO_PI, quarter, ALU.mult, ALU.add))
                link(V.tensor_scalar(turns, turns, ROUND, None, ALU.add))
                link(V.tensor_scalar(turns, turns, ROUND, None, ALU.subtract))
                link(V.scalar_tensor_tensor(arg, turns, -TURN[0], ang[:], ALU.mult, ALU.add))
                link(V.scalar_tensor_tensor(arg, turns, -TURN[1], arg, ALU.mult, ALU.add))
                link(V.scalar_tensor_tensor(arg, turns, -TURN[2], arg, ALU.mult, ALU.add))
                link(V.tensor_scalar(arg, arg, 2 * np.pi * quarter, 3.1415925, ALU.add, ALU.min))
                V.tensor_scalar(arg, arg, -3.1415925, None, ALU.max).then_inc(s_rt, 1)

            def row_splits(stage, half, last_only=False):
                name, l, nk = stage
                for k in range(0, nk, 2):
                    split_lo(W[(name, l, half, k)] + 3)

            first = ROWS[0]
            dve.wait_ge(s_ln, 32)
            for half in range(2):
                row_splits(first, half)
                for tb in range(TB):
                    row_wait(dve, first, half, tb)
                    xs = x[:, tb, half * 512:(half + 1) * 512]
                    if half or tb >= 2:
                        dve.wait_ge(dve_chain, chain[0] - 1)
                    V.tensor_tensor(prod[:, tb % 2, :], bank(4 * half + tb), gaterow[:, half * 512:(half + 1) * 512], ALU.mult).then_inc(row_read, 1)
                    dve.wait_ge(row_read, row_reads(first, half, tb))
                    k_ = step(V.scalar_tensor_tensor(xs, xs, ALPHA, prod[:, tb % 2, :], ALU.mult, ALU.add))
            dve.wait_ge(dve_chain, k_)
            layer_norm_rows(1)
            for tb in range(TB):
                dve.wait_ge(s_rstd, 4 + tb + 1)
                V.tensor_scalar(x[:, tb, :], x[:, tb, :], mv[:, 2 * tb:2 * tb + 1], rstd[:, tb:tb + 1],
                                ALU.subtract, ALU.mult).then_inc(s_xn, 1)
                dve.wait_ge(s_xn, 4 + tb + 1)
                link(V.tensor_tensor(x[:, tb, :], x[:, tb, :], lnrow[:, 0, :], ALU.mult))
                V.tensor_tensor(x[:, tb, :], x[:, tb, :], lnrow[:, 1, :], ALU.add).then_inc(x_ready, 1)

            def norm_rows(s):
                last = s == STAGES - 1

                def scaled(tb):
                    dve.wait_ge(s_rstd, 4 * s + tb + 1)
                    if last:
                        V.scalar_tensor_tensor(x[:, tb, :], x[:, tb, :], rstd[:, tb:tb + 1], frow[:], ALU.mult, ALU.mult).then_inc(s_xn, 1)
                    else:
                        V.tensor_scalar(xn2[:, tb % 2, :], x[:, tb, :], rstd[:, tb:tb + 1], None, ALU.mult).then_inc(s_xn, 1)

                if last:
                    dve.wait_ge(s_frow, 16)
                for tb in range(TB):
                    dve.wait_ge(s_ssq, 4 * (s - 2) + tb + 1)
                    V.tensor_scalar(msq[:, tb:tb + 1], ssq[:, tb:tb + 1], 1.0 / D, LN_EPS, ALU.mult, ALU.add).then_inc(s_ms, 1)
                    if tb:
                        scaled(tb - 1)
                scaled(TB - 1)

            def norm_lo(s, name, l):
                for ct in range(KT):
                    dve.wait_ge(h_hi, 8 * (s - 1) + ct + 1)
                    V.scalar_tensor_tensor(hT[:, 1, ct, :], bank(ct), col(name, 8 * l + ct), hT[:, 0, ct, :].bitcast(F),
                                           ALU.mult, ALU.subtract).then_inc(h_lo, 1)

            def add_rows(stage, scale):
                for half in range(2):
                    row_splits(stage, half)
                    for tb in range(TB):
                        row_wait(dve, stage, half, tb)
                        xs = x[:, tb, half * 512:(half + 1) * 512]
                        V.scalar_tensor_tensor(xs, bank(4 * half + tb), scale, xs, ALU.mult, ALU.add)\
                         .then_inc(x_ready if half else row_read, 1)

            for l in range(LAYERS):
                s = 2 + 2 * l
                norm_rows(s)
                norm_lo(s, "norm_mix", l)
                if l == 0:
                    dve.wait_ge(s_tab, 2)
                    link(V.tensor_scalar(table[:, 1, :], rt[:, 1, :], sign, None, ALU.mult))
                for key in (("sq", l, 0), ("sq", l, 1), ("sk", l, 0), ("sk", l, 1), ("sv", l, 0), ("sv", l, 1)):
                    split_lo(W[key] + 3)

                def rope(n_):
                    isq, g, j = n_ < 6, n_ // 2 % 3, n_ % 2
                    await_read(dve, DIL_KEYS(l)[n_])
                    if n_:
                        dve.wait_ge(rope_done, 12 * l + n_)
                    V.tensor_tensor(rot[:, 0, :], qraw[:, n_ % 2, :], table[:, 0, :], ALU.mult).then_inc(dve_chain, 1)
                    chain[0] += 1
                    dve.wait_ge(rot_ps, 12 * l + n_ + 1)
                    link(V.tensor_tensor(rot[:, 1, :], bank(7), table[:, 1, :], ALU.mult))
                    dst = (qd if isq else kd)[:, g, j, :]
                    if isq or g:
                        dst = dst.rearrange("p (r u) -> p u r", r=4)
                        a, b = (rot[:, i_, :].rearrange("p (u r) -> p u r", r=4) for i_ in range(2))
                    else:
                        a, b = rot[:, 0, :], rot[:, 1, :]
                    V.tensor_tensor(dst, a, b, ALU.add).then_inc(rope_done, 1)

                def sb_softplus(h):
                    for kb in range(TB):
                        dve.wait_ge(sb_l, 4 * (4 * l + h) + kb + 1)
                        w_ = SBO[kb + 1] - SBO[kb]
                        v = sbs[:, SBO[kb]:SBO[kb + 1]]
                        link(V.scalar_tensor_tensor(v, bank(2 + kb)[:, 0:w_], 0.0, sbl[:, SBO[kb]:SBO[kb + 1]], ALU.max, ALU.add))
                        v = sbs[:, SBO[kb]:SBO[kb] + P]
                        V.tensor_tensor(v, v, sbmul, ALU.mult).then_inc(sp_ready, 1)

                def sb_out(h):
                    dve.wait_ge(ob_hi, 4 * l + h + 1)
                    po = h % 2 * HEAD
                    V.tensor_tensor(obT[po:po + HEAD, h // 2, 1, :], bank(6)[po:po + HEAD, :],
                                    obT[po:po + HEAD, h // 2, 0, :].bitcast(F), ALU.subtract).then_inc(ob_lo, 1)

                for n_, key in enumerate(DIL_KEYS(l)):
                    split_lo(W[key] + 3)
                    if 1 <= n_ <= 12:
                        rope(n_ - 1)
                    h, ph = n_ // 4, n_ % 4
                    if ph == 0 and h >= 1:
                        sb_out(h - 1)
                    if ph == 0 and h < 4:
                        sb_softplus(h)

                def dil_max(u):
                    dve.wait_ge(s_ps, 16 * l + u + 1)
                    link(V.reduce_max(nmax[:, u:u + 1], psum[:, 2 * SEQ:2 * SEQ + 768], AX.X))
                    V.tensor_scalar(nmax[:, u:u + 1], nmax[:, u:u + 1], -1.0, None, ALU.mult).then_inc(max_done, 1)

                def dil_rden(u):
                    dve.wait_ge(p_ready, 16 * l + u + 1)
                    rd[u] = step(V.reciprocal(rden[:, u:u + 1], den[:, u:u + 1]))

                def dil_out(u):
                    r, h = u // 4, u % 4
                    dve.wait_ge(o_ps, 16 * l + u + 1)
                    dve.wait_ge(dve_chain, rd[u])
                    V.tensor_scalar(osb[:, r % 2, h * HEAD:(h + 1) * HEAD], bank(6)[:, 0:HEAD], rden[:, u:u + 1], None, ALU.mult).then_inc(o_ready, 1)

                def dil_oT(r):
                    dve.wait_ge(oa_hi, 4 * l + r + 1)
                    V.tensor_tensor(oaT[:, :, 1, r:SEQ:4], bank(7)[:, 0:256].rearrange("p (a b) -> p a b", a=2),
                                    oaT[:, :, 0, r:SEQ:4].bitcast(F), ALU.subtract).then_inc(oa_lo, 1)

                rd = {}
                for u in range(16):
                    split_lo(W[("gate", l, u)] + 3)
                    dil_max(u)
                    dil_rden(u)
                    if u >= 2:
                        dil_out(u - 2)
                    if u % 4 == 3 and u > 4:
                        dil_oT(u // 4 - 1)
                dil_out(14)
                for j in range(2):
                    split_lo(W[("w_proj_b_2", l, j)] + 3)
                    for mm in range(4):
                        m = 4 * j + mm
                        proj_wait(dve, pb_ps, "w_proj_b_2", l, j, mm)
                        if mm == 0:
                            await_read(dve, ("gate", l, 15))
                        V.scalar_tensor_tensor(gates[:, 8 + m, :], gates[:, 8 + m, :], 1.0, bank(m % 4), ALU.add, ALU.mult).then_inc(pb_f, 1)
                dil_out(15)
                dil_oT(3)
                for j in range(2):
                    split_lo(W[("w_proj_a_2", l, j)] + 3)
                    for mm in range(4):
                        m = 4 * j + mm
                        proj_wait(dve, pa_ps, "w_proj_a_2", l, j, mm)
                        V.scalar_tensor_tensor(gates[:, m, :], gates[:, m, :], 1.0, bank(m % 4), ALU.add, ALU.mult).then_inc(pa_f, 1)
                        dve.wait_ge(pa_f, 8 * l + m + 1)
                        V.tensor_tensor(gates[:, m, :], gates[:, m, :], gates[:, 8 + m, :], ALU.add).then_inc(mix_f, 1)
                        dve.wait_ge(mix_hi, 8 * l + m + 1)
                        V.tensor_tensor(hT[:, 1, m, :], gates[:, m, :], hT[:, 0, m, :].bitcast(F), ALU.subtract).then_inc(mix_lo, 1)
                add_rows(("w_out_2", l, KT), 0.5)

                norm_rows(s + 1)
                norm_lo(s + 1, "norm_ffn", l)
                link(V.memset(apad[:, :, 0:2], 0.0))
                for f2 in range(FT // 2):
                    for j in range(2):
                        f = 2 * f2 + j
                        key = ("up_a", l, f)
                        split_lo(W[key] + 3)
                        await_read(dve, key)
                        if FT * l + f:
                            dve.wait_ge(silu_done, FT * l + f)
                        cw = lambda k: col("conv_w", (3 * l + k) * FT + f)
                        link(V.tensor_scalar(facc[:], apad[:, j, 2:2 + SEQ], cw(2), col("conv_b", FT * l + f), ALU.mult, ALU.add))
                        link(V.scalar_tensor_tensor(facc[:], apad[:, j, 1:1 + SEQ], cw(1), facc[:], ALU.mult, ALU.add))
                        V.scalar_tensor_tensor(facc[:], apad[:, j, 0:SEQ], cw(0), facc[:], ALU.mult, ALU.add).then_inc(fconv, 1)
                    for j in range(2):
                        f = 2 * f2 + j
                        key = ("up_b", l, f)
                        split_lo(W[key] + 3)
                        w_wait_full(dve, key)
                        dve.wait_ge(silu_done, FT * l + f + 1)
                        V.tensor_tensor(fsil[:, j, :], bank(W_BANK[key]), fsil[:, j, :], ALU.mult).then_inc(dve_read, 1)
                        dve.wait_ge(ff_hi, FT * l + f + 1)
                        V.tensor_tensor(ff[:, f, 1, :], fsil[:, j, :], ff[:, f, 0, :].bitcast(F), ALU.subtract).then_inc(ff_lo, 1)
                add_rows(("w_down_2", l, FT), 1.0)
            norm_rows(STAGES - 1)

        @block.tensor
        def _(pe):
            M = nc.tensor.matmul
            reader = {}

            def take(*banks):
                for b in banks:
                    if b in reader:
                        pe.wait_ge(*reader.pop(b))

            def give(b, s_, value):
                reader[b] = (s_, value)

            def passes(out_, stat_hi, stat_lo, mov_hi, mov_lo, start, stop, **kw):
                M(out_, stat_hi, mov_hi, start=start, stop=False, **kw)
                M(out_, stat_hi, mov_lo, start=False, stop=False, **kw)
                return M(out_, stat_lo, mov_hi, start=False, stop=stop, **kw)

            def col_tile(key, xhi, xlo, ready=None):
                w = W[key]
                b = W_BANK[key]
                take(b)
                pe.wait_ge(w_lo, w + 1)
                hi, lo = whl_view(w, 0), whl_view(w, 1)
                for k in range(KT):
                    if ready is not None:
                        pe.wait_ge(ready[0], ready[1] + k + 1)
                    ins = passes(bank(b), hi[:, k, :], lo[:, k, :], xhi(k), xlo(k), k == 0, k == KT - 1)
                ins.then_inc(w_used, 1)
                if key in rcount:
                    give(b, *read_of(key))

            def row_tiles(stage, xhi, xlo, ready=None):
                name, l, nk = stage
                for half in range(2):
                    take(*range(4 * half, 4 * half + 4))
                    for k0 in range(0, nk, 2):
                        w = W[(name, l, half, k0)]
                        pe.wait_ge(w_lo, w + 1)
                        hi, lo = whl_view(w, 0), whl_view(w, 1)
                        for tb in range(TB):
                            ts = slice(tb * P, (tb + 1) * P)
                            for kk in range(2):
                                k = k0 + kk
                                if ready is not None and half == 0 and tb == 0:
                                    pe.wait_ge(ready[0], ready[1] + k + 1)
                                ins = passes(bank(4 * half + tb), xhi(k)[:, ts], xlo(k)[:, ts], hi[:, kk, :], lo[:, kk, :],
                                             k == 0, k == nk - 1)
                            if k0 == nk - 2 and tb < 3:
                                ins.then_inc(row_full, 1)
                        ins.then_inc(w_used, 1)
                    for tb in range(TB):
                        if half and l is not None:
                            give(4 * half + tb, x_ready, 4 * ROWS.index(stage) + tb + 1)
                        else:
                            give(4 * half + tb, row_read, row_reads(stage, half, tb))

            h_at = lambda hl: (lambda k: hT[:, hl, k, :])

            pe.wait_ge(s_cst, 32)
            pe.wait_ge(s_vec, 16 * NVEC_DMA)
            for g in range((NVEC + P - 1) // P):
                rows = min(P, NVEC - g * P)
                o_ = bank(g // 4)[:, g % 4 * P:g % 4 * P + rows]
                nc.tensor.transpose(o_, vstage[0:rows, g, :], ident[0:rows, 0:rows]).then_inc(s_vT, 1)
            give(0, s_ini, 7)
            give(1, s_vcol, 1)
            for tb in range(TB):
                pe.wait_ge(s_xn, tb + 1)
                for ct in range(KT - 1):
                    if tb == 0:
                        take(ct)
                    nc.tensor.transpose(bank(ct)[:, tb * P:(tb + 1) * P], xn1[:, tb, ct * P:(ct + 1) * P], ident)
            pe.wait_ge(s_cact, 1)
            pe.wait_ge(s_ada, 128)
            for m in range(16):
                lhs = ada[:, m // 2, :].rearrange("p (k n) -> p k n", k=KT)
                for k in range(KT):
                    ins = M(bank(7)[:, m:m + 1], lhs[:, k, m % 2 * P:(m % 2 + 1) * P], cact[:, k:k + 1], start=k == 0, stop=k == KT - 1)
            ins.then_inc(s_mod, 1)
            pe.wait_ge(s_modc, 1)
            for tb in range(TB):
                nc.tensor.transpose(bank(7)[:, tb * P:(tb + 1) * P], xn1[:, tb, (KT - 1) * P:], ident).then_inc(s_xT, 1)
            for ct in range(KT):
                give(ct, h_lo, ct + 1)

            for p in range(4):
                for key in PAIR_KEYS(p):
                    if key[0] == "pool_w":
                        w = W[key]
                        pe.wait_ge(w_lo, w + 1)
                        pe.wait_ge(pooled_lo, 2 * p + 2)
                        take(*POOL_BANK)
                        hi, lo = whl_view(w, 0), whl_view(w, 1)
                        for j in range(2):
                            for k in range(2):
                                ins = passes(bank(POOL_BANK[j]), hi[:, k, j * P:(j + 1) * P], lo[:, k, j * P:(j + 1) * P],
                                             poolhl[:, k, 0, :], poolhl[:, k, 1, :], k == 0, k == 1)
                            give(POOL_BANK[j], ya_f, 2 * p + j + 1)
                        ins.then_inc(w_used, 1)
                        continue
                    col_tile(key, h_at(0), h_at(1), (h_lo, 0) if key == ("w_in", CA) else None)
                    if key == ("w_in", CB + 1):
                        pe.wait_ge(s_adag, 64)
                        pe.wait_ge(s_crep, 8)
                        take(6, 7)
                        for q in range(4):
                            for k in range(KT):
                                ins = M(bank(6 + q // 2)[:, q % 2 * 256:q % 2 * 256 + 256], crep[:, k, :],
                                        ada[:, q, k * 256:(k + 1) * 256], start=k == 0, stop=k == KT - 1)
                        ins.then_inc(s_gp, 1)
                        give(6, s_gate, 1)
                        give(7, s_gate, 1)

            operand = [(lambda k: yahl[:, 0, k, :], lambda k: yahl[:, 1, k, :], (ya_lo, 0)),
                       (lambda k: ybhi[:, k, :], lambda k: yblo[:, k, :], (yb_lo, 0)),
                       (lambda k: ychi[:, k, :], lambda k: yclo[:, k, :], (yc_lo, 0))]
            for i in range(3):
                for q in range(4):
                    if i == 1 and q == 1:
                        pe.wait_ge(hc_done, KT)
                        take(STAT_BANK)
                        for k in range(KT):
                            ins = M(bank(STAT_BANK), onesd[:], hc[:, k, :], start=k == 0, stop=k == KT - 1)
                        ins.then_inc(mean_ps, 1)
                        give(STAT_BANK, cen, KT)
                    if i == 1 and q == 2:
                        take(STAT_BANK)
                        for k in range(KT):
                            pe.wait_ge(sqd, k + 1)
                            ins = M(bank(STAT_BANK), onesd[:], sq[:, k, :], start=k == 0, stop=k == KT - 1)
                        ins.then_inc(var_ps, 1)
                        give(STAT_BANK, ve, 1)
                    for j in range(2):
                        col_tile(("w_in", MG + 8 * i + 2 * q + j), h_at(0), h_at(1))
                    for j in range(2):
                        hi_, lo_, ready = operand[i]
                        col_tile(("w_branch", i, 2 * q + j), hi_, lo_, ready if q == 0 and j == 0 else None)
            row_tiles(ROWS[0], lambda k: mhi[:, k, :], lambda k: mlo[:, k, :], (m_lo, 0))

            def norm_transposes(s):
                for tb in range(TB):
                    pe.wait_ge(s_xn, 4 * s + tb + 1)
                    for ct in range(KT):
                        if tb == 0:
                            take(ct)
                        ins = nc.tensor.transpose(bank(ct)[:, tb * P:(tb + 1) * P], xn2[:, tb % 2, ct * P:(ct + 1) * P], ident)
                    ins.then_inc(s_xT, 1)
                for ct in range(KT):
                    give(ct, h_lo, 8 * (s - 1) + ct + 1)

            for l in range(LAYERS):
                s = 2 + 2 * l
                norm_transposes(s)

                def token_tile(key, strided):
                    w = W[key]
                    b = W_BANK[key]
                    first_, last_ = key[-1] == 0, key[-1] == 1
                    if first_:
                        take(b, b + 1)
                    pe.wait_ge(w_lo, w + 1)
                    hi, lo = whl_view(w, 0), whl_view(w, 1)
                    for tb in range(TB):
                        ts = slice(tb, SEQ, 4) if strided else slice(tb * P, (tb + 1) * P)
                        o_ = bank(b + tb // 2)[:, tb % 2 * 256:tb % 2 * 256 + 256]
                        for kk in range(4):
                            k = 4 * key[-1] + kk
                            ins = passes(o_, hT[:, 0, k, ts], hT[:, 1, k, ts], hi[:, kk, :], lo[:, kk, :],
                                         k == 0 and tb % 2 == 0, last_ and kk == 3, skip_group_check=True)
                    ins.then_inc(w_used, 1)
                    if last_:
                        give(b, *read_of(key))
                        give(b + 1, *read_of(key))

                for n_, key in enumerate([("sq", l, 0), ("sq", l, 1), ("sk", l, 0), ("sk", l, 1)]):
                    col_tile(key, h_at(0), h_at(1), (h_lo, 8 * (s - 1)) if n_ == 0 else None)
                token_tile(("sv", l, 0), False)
                token_tile(("sv", l, 1), False)

                def sb_scores(h):
                    po = h % 2 * HEAD
                    rows = slice(po, po + HEAD)
                    await_read(pe, ("sq", l, 1))
                    await_read(pe, ("sk", l, 1))
                    for kb in range(TB):
                        take(2 + kb)
                        M(bank(2 + kb)[:, 0:SEQ - kb * P], sbk[rows, h // 2, kb * P:(kb + 1) * P], sbq[rows, h // 2, kb * P:],
                          start=True, stop=True, skip_group_check=True).then_inc(z_ps, 1)

                def sb_exponents(h):
                    for kb in range(TB):
                        n0 = 4 * (4 * l + h)
                        if kb == 0:
                            pe.wait_ge(sp_ready, n0 + 4)
                        for jb in range(kb, TB):
                            M(bank(2 + kb)[:, (jb - kb) * P:SEQ - kb * P], negtri if jb == kb else negones[:], sbs[:, SBO[jb]:SBO[jb + 1]],
                              start=False, stop=False, skip_group_check=True)
                        M(bank(2 + kb)[:, 0:P], identb[:], sbaddb[:], start=False, stop=True, skip_group_check=True).then_inc(e_ps, 1)
                        give(2 + kb, sb_attn, n0 + kb + 1)

                def sb_values(h):
                    po = h % 2 * HEAD
                    take(6)
                    if h == 0:
                        await_read(pe, ("sv", l, 1))
                    for kb in range(TB):
                        pe.wait_ge(sb_attn, 4 * (4 * l + h) + kb + 1)
                        ins = M(bank(6)[po:po + HEAD, kb * P:], sbv[:, kb, h * HEAD:(h + 1) * HEAD], sba[:, SBO[kb]:SBO[kb + 1]],
                                start=kb == 0, stop=kb == TB - 1, skip_group_check=True)
                    ins.then_inc(sbo_ps, 1)
                    give(6, ob_lo, 4 * l + h + 1)

                for n_, key in enumerate(DIL_KEYS(l)):
                    if key[0] == "dv":
                        token_tile(key, key[2] > 0)
                    else:
                        col_tile(key, h_at(0), h_at(1))
                    if 1 <= n_ <= 12:
                        await_read(pe, DIL_KEYS(l)[n_ - 1])
                        take(7)
                        M(bank(7), swapm, qraw[:, (n_ - 1) % 2, :], start=True, stop=True).then_inc(rot_ps, 1)
                        give(7, rope_done, 12 * l + n_)
                    h, ph = n_ // 4, n_ % 4
                    if ph == 0 and h >= 1:
                        sb_values(h - 1)
                    if ph == 0 and h < 4:
                        sb_scores(h)
                    if ph == 2 and h < 4:
                        sb_exponents(h)

                def dil_scores(u):
                    r, h = u // 4, u % 4
                    po = h % 2 * HEAD
                    rows = slice(po, po + HEAD)
                    if u == 0:
                        pe.wait_ge(rope_done, 12 * l + 12)
                    take(2, 3)
                    for g in range(3):
                        o_ = psum[:, 2 * SEQ:3 * SEQ] if g == 0 else psum[:, 3 * SEQ + (g - 1) * P:3 * SEQ + g * P]
                        keys = kd[rows, 0, h // 2, :] if g == 0 else kd[rows, g, h // 2, r * P:(r + 1) * P]
                        mask = bandb[:, 3 - r:3 - r + SEQ] if g == 0 else ownb[:, (g - 1) * P:g * P]
                        M(o_, qd[rows, g, h // 2, r * P:(r + 1) * P], keys, start=True, stop=False)
                        ins = M(o_, identb[:], mask, start=False, stop=True)
                    ins.then_inc(s_ps, 1)
                    give(2, p_ready, 16 * l + u + 1)
                    give(3, p_ready, 16 * l + u + 1)

                def dil_transposes(u):
                    pe.wait_ge(p_ready, 16 * l + u + 1)
                    take(4, 5)
                    for b in range(6):
                        ins = nc.tensor.transpose(psum[:, 4 * SEQ + b * P:4 * SEQ + (b + 1) * P], prob[:, u % 2, b * P:(b + 1) * P], ident)
                    ins.then_inc(pT_ps, 1)
                    give(4, pT_ready, 16 * l + u + 1)
                    give(5, pT_ready, 16 * l + u + 1)

                def dil_values(u):
                    r, h = u // 4, u % 4
                    pe.wait_ge(pT_ready, 16 * l + u + 1)
                    take(6)
                    hs = slice(h * HEAD, (h + 1) * HEAD)
                    vals = [vd[:, 0, b, hs] for b in range(TB)] + [vd[:, 1, r, hs], vd[:, 2, r, hs]]
                    for b, v in enumerate(vals):
                        ins = M(bank(6)[:, 0:HEAD], probT[:, u % 2, b * P:(b + 1) * P], v, start=b == 0, stop=b == 5)
                    ins.then_inc(o_ps, 1)
                    give(6, o_ready, 16 * l + u + 1)

                def dil_oT(r):
                    pe.wait_ge(o_ready, 16 * l + 4 * r + 4)
                    take(7)
                    for ct in range(2):
                        ins = nc.tensor.transpose(bank(7)[:, ct * P:(ct + 1) * P], osb[:, r % 2, ct * P:(ct + 1) * P], ident)
                    ins.then_inc(oT_ps, 1)
                    give(7, oa_lo, 4 * l + r + 1)

                await_read(pe, ("dv", l, 2, 1))
                dil_scores(0)
                for u in range(16):
                    col_tile(("gate", l, u), h_at(0), h_at(1))
                    dil_transposes(u)
                    if u < 15:
                        dil_scores(u + 1)
                    if u:
                        dil_values(u - 1)
                    if u % 4 == 2 and u > 4:
                        dil_oT(u // 4 - 1)

                def projection(name, oT, s_full, s_read):
                    for j in range(2):
                        w = W[(name, l, j)]
                        pe.wait_ge(w_lo, w + 1)
                        hi, lo = whl_view(w, 0), whl_view(w, 1)
                        for mm in range(4):
                            m = 4 * j + mm
                            take(m % 4)
                            for k in range(2):
                                ins = passes(bank(m % 4), hi[:, k, mm * P:(mm + 1) * P], lo[:, k, mm * P:(mm + 1) * P],
                                             oT[:, k, 0, :], oT[:, k, 1, :], k == 0, k == 1)
                            if mm < 3:
                                ins.then_inc(s_full, 1)
                            give(m % 4, s_read, 8 * l + m + 1)
                        ins.then_inc(w_used, 1)

                pe.wait_ge(ob_lo, 4 * l + 4)
                projection("w_proj_b_2", obT, pb_ps, pb_f)
                dil_values(15)
                dil_oT(3)
                pe.wait_ge(oa_lo, 4 * l + 4)
                projection("w_proj_a_2", oaT, pa_ps, pa_f)
                row_tiles(("w_out_2", l, KT), h_at(0), h_at(1), (mix_lo, 8 * l))
                norm_transposes(s + 1)
                for f2 in range(FT // 2):
                    for name in ("up_a", "up_b"):
                        for j in range(2):
                            key = (name, l, 2 * f2 + j)
                            col_tile(key, h_at(0), h_at(1), (h_lo, 8 * s) if key == ("up_a", l, 0) else None)
                row_tiles(("w_down_2", l, FT), lambda k: ff[:, k, 0, :], lambda k: ff[:, k, 1, :], (ff_lo, FT * l))


_INS = ["x", "c", "w_ada", "b_ada", "w_in", "b_in", "pool_w", "pool_scale", "sc_w", "sc_b", "cf_w", "cf_b", "cf_ln_g",
        "cf_ln_b", "w_branch", "w_out", "ln_g", "ln_b", "positions_2", "norm_mix_2", "w_in_2", "b_gate_2", "w_proj_a_2",
        "w_proj_b_2", "w_out_2", "norm_ffn_2", "w_up_2", "conv_w_2", "conv_b_2", "w_down_2", "norm_final_2"]


def kernel(**inputs):
    import concourse.bacc as bacc
    from concourse.bass_utils import run_bass_kernel_spmd

    nc = bacc.Bacc("TRN2", target_bir_lowering=False, num_devices=1)
    arrays = {f"in_{name}": np.ascontiguousarray(inputs[name]) for name in _INS}
    arrays["in_consts"] = shape_constants()
    t = {name[3:]: nc.dram_tensor(name, a.shape, mybir.dt.from_np(a.dtype), kind="ExternalInput").ap() for name, a in arrays.items()}
    out = nc.dram_tensor("out", (1, SEQ, D), mybir.dt.float32, kind="ExternalOutput").ap()
    build(nc, t, out)
    r = run_bass_kernel_spmd(nc, [arrays], core_ids=[0])
    return r.results[0]["out"]
```

```python
import numpy as np
from contextlib import ExitStack
import concourse.bass as bass
from concourse import mybir

P = 128
D = 1024
SEQ = 512
KT = D // P
TB = SEQ // P
LAYERS = 2
POOL_WINDOWS = (2, 4, 8, 16)
CF_TAPS = 31
LN_EPS = 1e-5
ALPHA = 2.0 ** 0.25
D_FF = 2816
FT = D_FF // P
HEAD = 64
ROPE_DIM = HEAD // 4
ROPE_THETA = 500000.0
MASK = -1e30
TWO_PI = 2.0 * np.pi

VECS = [("b_in", 96), ("pool_scale", 8), ("sc_w", 24), ("sc_b", 8), ("cf_b", 8), ("cf_ln_g", 8),
        ("cf_ln_b", 8), ("c", 8), ("b_ada", 24), ("cf_w", CF_TAPS * 8), ("norm_mix", 16),
        ("b_gate", 32), ("norm_ffn", 16), ("conv_w", 2 * 3 * FT), ("conv_b", 2 * FT)]
VOFF, _n = {}, 0
for _name, _rows in VECS:
    VOFF[_name] = _n
    _n += _rows
NVEC = _n
AV, AG, BB, BC, BH, BG, CA, CB, CG, MG = (8 * i for i in range(10))

CONSTS = [("ident", 128), ("negtri", 128), ("swap", 128), ("sbmul", 128), ("corr", 64), ("freq", 1),
          ("sign", 1), ("band", 516), ("own", 256), ("sbadd", 128)]
COFF, _n = {}, 0
for _name, _rows in CONSTS:
    COFF[_name] = _n
    _n += _rows
NCONST = _n
NKEEP = COFF["band"]


def shape_constants():
    out = np.zeros((P, NCONST), np.float32)
    i = np.arange(P)

    def put(name, value):
        value = np.asarray(value, np.float32).reshape(P, -1)
        out[:, COFF[name]:COFF[name] + value.shape[1]] = value

    put("ident", np.eye(P))
    put("negtri", -(i[:, None] >= i[None, :]).astype(np.float32))
    swap = np.zeros((P, P))
    for p in range(P):
        if p % HEAD < ROPE_DIM:
            swap[p - p % ROPE_DIM + (p % ROPE_DIM + ROPE_DIM // 2) % ROPE_DIM, p] = 1.0
    put("swap", swap)
    put("sbmul", (i[:, None] < i[None, :]).astype(np.float32))
    put("sbadd", np.where(i[:, None] < i[None, :], 0.0, MASK))
    t = np.arange(16)
    put("corr", np.tile(np.concatenate([w / np.minimum(t + 1, w) for w in POOL_WINDOWS])[None], (P, 1)))
    inv = (np.float32(ROPE_THETA) ** (-np.arange(0, ROPE_DIM, 2, dtype=np.float32) / np.float32(ROPE_DIM)))
    put("freq", np.where(i % HEAD < ROPE_DIM, inv[i % (ROPE_DIM // 2)], 0.0))
    put("sign", np.where(i % ROPE_DIM < ROPE_DIM // 2, -1.0, 1.0))
    gap = 4 * i[:, None] - (np.arange(516)[None, :] - 3)
    put("band", np.where((gap >= 0) & (gap <= 128), 0.0, MASK))
    gap = i[:, None] - i[None, :]
    put("own", np.concatenate([np.where(gap >= 0, 0.0, MASK),
                               np.where((gap >= 0) & (gap % 4 == 0), 0.0, MASK)], 1))
    return out


def weight_plan():
    chunks, number = [], {}

    def add(tensor, key, keys, words):
        pieces = []
        for k in keys:
            number[k] = len(number)
            pieces.append((k, words))
        chunks.append((tensor, key, pieces))

    def cols(tensor, sec, pair):
        add(tensor, (tensor, sec, pair), [(tensor, sec + 2 * pair + j) for j in range(2)], 1024)

    for p in range(4):
        for sec in (CA, CB, CG, AV, AG):
            cols("w_in", sec, p)
        add("pool_w", ("pool_w", p), [("pool_w", p)], 512)
        for sec in (BC, BH, BB, BG):
            cols("w_in", sec, p)
    for i in range(3):
        for q in range(4):
            cols("w_in", MG + 8 * i, q)
            add("w_branch", ("w_branch", i, q), [("w_branch", i, 2 * q + j) for j in range(2)], 1024)

    def rows(tensor, l, nk):
        for half in range(2):
            for k0 in range(0, nk, 4):
                n = min(4, nk - k0)
                add(tensor, (tensor, l, half, k0, n),
                    [(tensor, l, half, k0 + 2 * j) for j in range(n // 2)], 1024)

    rows("w_out", None, KT)
    for l in range(LAYERS):
        for name, sec in (("sq", 9), ("sk", 10)):
            add("w_in_2", ("w_in_2", l, sec), [(name, l, j) for j in range(2)], 1024)
        add("w_in_2", ("w_in_2v", l, 11), [("sv", l, j) for j in range(2)], 1024)
        for name, sec in (("dq", 0), ("dk", 3)):
            for g in range(3):
                add("w_in_2", ("w_in_2", l, sec + g), [(name, l, g, j) for j in range(2)], 1024)
        for g in range(3):
            add("w_in_2", ("w_in_2v", l, 6 + g), [("dv", l, g, j) for j in range(2)], 1024)
        for q in range(8):
            add("w_in_2", ("w_in_2", l, 12 + q), [("gate", l, 2 * q + j) for j in range(2)], 1024)
        for name in ("w_proj_b_2", "w_proj_a_2"):
            add(name, (name, l), [(name, l, j) for j in range(2)], 1024)
        rows("w_out_2", l, KT)
        for f in range(FT // 2):
            for name, sec in (("up_a", 0), ("up_b", FT // 2)):
                add("w_up_2", ("w_up_2", l, sec + f), [(name, l, 2 * f + j) for j in range(2)], 1024)
        rows("w_down_2", l, FT)
    return chunks, number


def build(nc, t, out):
    F = mybir.dt.float32
    R = mybir.dt.float32r
    BF = mybir.dt.bfloat16
    I32 = mybir.dt.int32
    ALU = mybir.AluOpType
    ACT = mybir.ActivationFunctionType
    AX = mybir.AxisListType

    chunks, W = weight_plan()
    pieces = []
    for c, (_, _, ps) in enumerate(chunks):
        for j, (_, words) in enumerate(ps):
            pieces.append((c, j, words))
    last_piece = []
    for c, (_, _, ps) in enumerate(chunks):
        last_piece.append(W[ps[-1][0]])
    NP_ = len(pieces)

    W_BANK = {}
    POOL_BANK = (6, 7)
    STAT_BANK = 6
    STAGES = 3 + 2 * LAYERS
    SETUP = 11
    SBO = [0, 512, 896, 1152, 1280]
    TURN = (6.28125, 2029.0 / 2 ** 20, TWO_PI - 6.28125 - 2029.0 / 2 ** 20)
    ROUND = 1.5 * 2 ** 23

    def PAIR_KEYS(p):
        keys = [("w_in", sec + 2 * p + j) for sec in (CA, CB, CG, AV, AG) for j in range(2)]
        keys.append(("pool_w", p))
        return keys + [("w_in", sec + 2 * p + j) for sec in (BC, BH, BB, BG) for j in range(2)]

    def DIL_KEYS(l):
        return [(name, l, g, j) for name in ("dq", "dk", "dv") for g in range(3) for j in range(2)]

    count = 0
    for key in W:
        if key[0] in ("w_in", "w_branch"):
            W_BANK[key] = count % 6
            count += 1
        elif key[0] in ("sq", "sk"):
            W_BANK[key] = key[-1] + 2 * (key[0] == "sk")
        elif key[0] in ("dq", "dk", "gate"):
            W_BANK[key] = key[-1] % 2
        elif key[0] == "sv":
            W_BANK[key] = 4
        elif key[0] == "dv":
            W_BANK[key] = 4 if key[2] == 2 else 0
        elif key[0] in ("up_a", "up_b"):
            W_BANK[key] = (2 * key[2] + (key[0] == "up_b") * 2 - key[2] % 2) % 8

    base = (nc.sbuf_base + 63) // 64 * 64
    top = nc.sbuf_usable_end
    at = [base]

    def keep(name, shape, dt=F):
        size = int(np.prod(shape[1:])) * (2 if dt == BF else 4)
        size = (size + 31) // 32 * 32
        h = nc.alloc_sbuf_tensor_at(name, shape, dt, offset=at[0])
        at[0] += size
        return h

    x = keep("x", [P, TB, D])
    hT = keep("hT", [P, 2, KT, SEQ], R)
    raw = keep("raw", [P, 2, 2048])
    whl = keep("whl", [P, 4, 2, 1024], R)
    cst_at = at[0]
    cst = keep("cst", [P, NKEEP])
    tri_at = at[0]
    onesd = keep("onesd", [P, P])
    negones = keep("negones", [P, P])
    identb = keep("identb", [P, P], BF)
    bandb = keep("bandb", [P, 516], BF)
    ownb = keep("ownb", [P, 256], BF)
    sbaddb = keep("sbaddb", [P, P], BF)
    vcol_at = at[0]
    vcol = keep("vcol", [P, NVEC])
    halfb = keep("halfb", [P, 96 + 32])
    stat = keep("stat", [P, 160])
    table = keep("table", [P, 2, SEQ])
    arena = at[0]
    negtri_r = nc.alloc_sbuf_tensor_at("negtri_r", [P, P], R, offset=tri_at)
    swap_r = nc.alloc_sbuf_tensor_at("swap_r", [P, P], R, offset=cst_at + 4 * COFF["negtri"])
    negones_r = nc.alloc_sbuf_tensor_at("negones_r", [P, P], R, offset=vcol_at)

    def over(name, offset, shape, dt=F):
        size = int(np.prod(shape[1:])) * (2 if dt == BF else 4)
        assert arena + offset + size <= top, (name, arena + offset + size - top)
        return nc.alloc_sbuf_tensor_at(name, shape, dt, offset=arena + offset)

    K = 1024
    ada = over("ada", 0, [P, 8, 2048])
    vstage = over("vstage", 64 * K, [P, 6, P])
    cstage = over("cstage", 68 * K, [P, NCONST - NKEEP])
    adsum = over("adsum", 72 * K, [P, 8, 256])
    utmp = over("utmp", 64 * K, [P, 2, SEQ])
    xn1 = over("xn1", 82 * K, [P, TB, D])
    yahl = over("yahl", 0, [P, 2, KT, SEQ], R)
    sag = over("sag", 16 * K, [P, KT, SEQ])
    ybf = over("ybf", 32 * K, [P, KT, SEQ])
    hc = over("hc", 48 * K, [P, KT, SEQ])
    cg = over("cg", 64 * K, [P, KT, SEQ])
    o = 80 * K
    glu = over("glu", o, [P, 2, SEQ + CF_TAPS - 1])
    acc1 = over("acc1", o + 4352, [P, SEQ])
    vpad = over("vpad", o + 6400, [P, 16 + SEQ])
    poolhl = over("poolhl", o + 8512, [P, 2, 2, SEQ], R)
    sbuf1 = over("sbuf1", o + 8512, [P, 2, 2 * SEQ])
    sbg = over("sbg", o + 8512, [P, 2, SEQ])
    yaf = over("yaf", o + 16704, [P, 16 + SEQ])
    mT = over("mT", o, [P, KT, SEQ])
    tg = over("tg", o + 16384, [P, SEQ])
    tg2 = over("tg2", 8 * K, [P, 2, SEQ])
    ybhi = over("ybhi", 0, [P, KT, SEQ], R)
    yblo = over("yblo", 32 * K, [P, KT, SEQ], R)
    sq = over("sq", 16 * K, [P, KT, SEQ])
    ychi = over("ychi", 16 * K, [P, KT, SEQ], R)
    yclo = over("yclo", 48 * K, [P, KT, SEQ], R)
    mhi = over("mhi", 64 * K, [P, KT, SEQ], R)
    mlo = over("mlo", 32 * K, [P, KT, SEQ], R)
    lnrow = over("lnrow", 0, [P, 2, D])
    prod = over("prod", 8 * K, [P, 2, SEQ])
    pos_i = over("pos_i", 12 * K, [P, SEQ], I32)
    ang = over("ang", 14 * K, [P, SEQ])
    rt = over("rt", 16 * K, [P, 3, SEQ])
    qd = over("qd", 0, [P, 3, 2, SEQ])
    kd = over("kd", 12 * K, [P, 3, 2, SEQ])
    vd = over("vd", 24 * K, [P, 3, TB, 256])
    sbq = over("sbq", 36 * K, [P, 2, SEQ])
    sbk = over("sbk", 40 * K, [P, 2, SEQ])
    sbv = over("sbv", 44 * K, [P, TB, 256])
    prob = over("prob", 36 * K, [P, 2, 768])
    probT = over("probT", 42 * K, [P, 2, 768])
    gates = over("gates", 48 * K, [P, 16, SEQ])
    sbl = over("sbl", 64 * K, [P, 1280])
    sbs = over("sbs", 69 * K, [P, 1280])
    sphi = over("sphi", 64 * K, [P, 1280], R)
    splo = over("splo", 69 * K, [P, 1280], R)
    sba = over("sba", 74 * K, [P, 1280])
    oaT = over("oaT", 80 * K, [P, 2, 2, SEQ], R)
    obT = over("obT", 88 * K, [P, 2, 2, SEQ], R)
    qraw = over("qraw", 80 * K, [P, 2, SEQ])
    rot = over("rot", 84 * K, [P, 2, SEQ])
    qhl = over("qhl", 48 * K, [P, 2, 2, SEQ], R)
    osb = over("osb", 96 * K, [P, 2, 256])
    ff = over("ff", 0, [P, FT, 2, SEQ], R)
    xn2 = over("xn2", 88 * K, [P, 2, D])
    apad = over("apad", 88 * K, [P, 2, SEQ + 2])
    facc = over("facc", 88 * K + 4128, [P, SEQ])
    fsil = over("fsil", 88 * K + 6176, [P, 2, SEQ])
    frow = over("frow", 92 * K, [P, D])
    xn4 = over("xn4", 80 * K, [P, TB, D])

    ident = cst[:, COFF["ident"]:COFF["ident"] + P]
    negtri = cst[:, COFF["negtri"]:COFF["negtri"] + P]
    swapm = cst[:, COFF["swap"]:COFF["swap"] + P]
    sbmul = cst[:, COFF["sbmul"]:COFF["sbmul"] + P]
    freq = cst[:, COFF["freq"]:COFF["freq"] + 1]
    sign = cst[:, COFF["sign"]:COFF["sign"] + 1]

    gaterow = table[:, :, :].rearrange("p a b -> p (a b)")

    def col(name, i):
        return vcol[:, VOFF[name] + i:VOFF[name] + i + 1]

    bnst, mv, ssq, msq, rstd, neghalf = stat[:, 0:48], stat[:, 48:56], stat[:, 56:60], stat[:, 60:64], stat[:, 64:68], stat[:, 68:72]
    modc, cact, nmax, den, rden = stat[:, 72:88], stat[:, 88:96], stat[:, 96:112], stat[:, 112:128], stat[:, 128:144]

    ctx = ExitStack()
    with ctx:
        psum = ctx.enter_context(nc.psum_tensor("psum", [P, 8 * SEQ], F))

        def bank(b):
            return psum[:, b * SEQ:(b + 1) * SEQ]

        def sem(name):
            return ctx.enter_context(nc.semaphore(name))

        raw_in = [sem("raw_in0"), sem("raw_in1")]
        w_hi, w_lo, w_used = sem("w_hi"), sem("w_lo"), sem("w_used")
        s_x, s_vec, s_vec2, s_cst, s_adag, s_bcast = (sem(n) for n in ("x_in", "vec_in", "vec2_in", "cst_in", "adag_in", "bcast_in"))
        s_ada = [sem(f"ada_in{q}") for q in range(8)]
        s_vT, s_vcol, s_mod, s_modc, s_gp, s_gate = (sem(n) for n in ("vecT", "vcol_ready", "mod_psum", "modc_ready", "gate_psum", "gate_ready"))
        s_ini, s_cact, s_adsum, s_gsum = sem("setup_done"), sem("cact_ready"), sem("ada_summed"), sem("adag_summed")
        s_ssq, s_ms, s_rstd, s_xn, s_xT, h_hi, h_lo = (sem(n) for n in ("sumsq", "ms_ready", "rstd_ready", "xn_ready", "xT_done", "h_hi", "h_lo"))
        x_ready, h_f = sem("x_ready"), sem("h_gained")
        act_read, dve_read = sem("act_read"), sem("dve_read")
        pooled_f, pooled_hi, pooled_lo, ya_f, ya_hi, ya_lo, yb_f, hc_done = (sem(n) for n in ("pooled_f", "pooled_hi", "pooled_lo", "ya_f", "ya_hi", "ya_lo", "yb_f", "hc_done"))
        m_part, yb_hi, yb_lo, mean_ps, sqd, cen, var_ps, ve, sqr, nrm, ycs, ycf, yc_hi, yc_lo, m_hi, m_lo = (
            sem(n) for n in ("m_part", "yb_hi", "yb_lo", "mean_psum", "squared", "centred", "var_psum", "var_eps", "std_ready",
                             "normed", "yc_silu", "yc_f", "yc_hi", "yc_lo", "m_hi", "m_lo"))
        row_full, row_read, s_ln, s_rt, s_pos, s_tab = (sem(n) for n in ("row_full", "row_read", "lnrow_in", "rot_steps", "pos_in", "tables_ready"))
        sp_hi, sp_lo, q_lo = sem("sp_hi"), sem("sp_lo"), sem("q_lo")
        rot_ps, rope_done, z_ps, sb_abs, sb_l, sp_ready, e_ps, sb_attn, sbo_ps, ob_hi, ob_lo = (
            sem(n) for n in ("rot_psum", "rope_done", "z_psum", "sb_abs", "sb_log", "sp_ready", "e_psum", "sb_attn",
                             "sbo_psum", "ob_hi", "ob_lo"))
        s_ps, max_done, p_ready, pT_ps, pT_ready, o_ps, o_ready, oT_ps, oa_hi, oa_lo = (
            sem(n) for n in ("s_psum", "max_done", "p_ready", "pT_psum", "pT_ready", "o_psum", "o_ready", "oT_psum", "oa_hi", "oa_lo"))
        pb_ps, pb_f, pa_ps, pa_f, mix_f, mix_hi, mix_lo = (sem(n) for n in ("pb_psum", "pb_f", "pa_psum", "pa_f", "mix_f", "mix_hi", "mix_lo"))
        fconv, silu_done, ff_hi, ff_lo = (sem(n) for n in ("ffn_conv", "silu_done", "ff_hi", "ff_lo"))
        s_out, s_frow = sem("out_done"), sem("frow_in")
        dve_chain, act_chain, pool_chain = sem("dve_chain"), sem("act_chain"), sem("pool_chain")

        READER = {CA: "dve", CB: "act", CG: "act", AV: "act", AG: "act", BC: "act", BH: "dve", BB: "dve", BG: "act"}
        RSEM = {"act": act_read, "dve": dve_read}
        rcount = {}
        n = {"act": 0, "dve": 0}
        for key in W:
            who = None
            if key[0] == "w_in":
                sec = key[1] // 8 * 8
                who = READER.get(sec, "act")
            elif key[0] == "w_branch":
                who = "dve"
            elif key[0] in ("sq", "sk", "dq", "dk", "gate"):
                who = "act"
            elif key[0] in ("sv", "dv"):
                who = "act" if key[-1] == 1 else None
            elif key[0] == "up_a":
                who = "act"
            elif key[0] == "up_b":
                who = "dve"
            if who:
                n[who] += 1
                rcount[key] = (who, n[who])

        def read_of(key):
            who, v = rcount[key]
            return RSEM[who], v

        def await_read(eng, key):
            s, v = read_of(key)
            eng.wait_ge(s, v)

        def w_wait_full(eng, key):
            eng.wait_ge(w_used, W[key] + 1)

        def raw_view(w):
            c, j, words = pieces[w]
            tensor, key, ps = chunks[c]
            r = raw[:, c % 2, :]
            kind = ps[0][0][0]
            if kind == "pool_w":
                return r[:, 0:512].rearrange("p (a b) -> p a b", a=2)
            if kind in ("w_proj_a_2", "w_proj_b_2"):
                return r.rearrange("p (a b) -> p a b", a=2)[:, :, j * 512:(j + 1) * 512]
            if kind in ("w_out", "w_out_2", "w_down_2"):
                return r[:, j * 1024:(j + 1) * 1024].rearrange("p (a b) -> p a b", a=2)
            if kind in ("sv", "dv"):
                return r[:, j * 1024:(j + 1) * 1024].rearrange("p (a b) -> p a b", a=4)
            return r.rearrange("p (a b) -> p a b", a=8)[:, :, j * P:(j + 1) * P]

        def whl_view(w, part):
            a = raw_view(w).shape[1]
            n_ = pieces[w][2]
            return whl[:, w % 4, part, 0:n_].rearrange("p (a b) -> p a b", a=a)

        def split_hi(w):
            if w >= NP_:
                return
            c = pieces[w][0]
            nc.scalar.wait_ge(raw_in[c % 2], 16 * (c // 2 + 1))
            if w >= 4:
                nc.scalar.wait_ge(w_used, w - 3)
            nc.scalar.activation(whl_view(w, 0), raw_view(w), ACT.Copy).then_inc(w_hi, 1)

        def split_lo(w):
            if w >= NP_:
                return
            nc.vector.wait_ge(w_hi, w + 1)
            nc.vector.tensor_tensor(whl_view(w, 1), raw_view(w), whl_view(w, 0).bitcast(F),
                                    ALU.subtract).then_inc(w_lo, 1)

        ROWS = [("w_out", None, KT)] + [s for l in range(LAYERS) for s in (("w_out_2", l, KT), ("w_down_2", l, FT))]

        def resident(stage):
            name, l, nk = stage
            return W[(name, l, 1, nk - 8)]

        def lead_keys(stage):
            name, l, nk = stage
            return [(name, l, 0, k) for k in range(0, nk, 2)] + [(name, l, 1, k) for k in range(0, nk - 6, 2)]

        ORDER = [(0, tb) for tb in range(TB)]
        ORDER += [(1, 0), (1, 1), (2, 0), (1, 2), (2, 1), (1, 3), (2, 2), (2, 3)]
        ORDER += [(s_, tb) for s_ in range(3, STAGES) for tb in range(TB)]
        root_at = {st: i_ + 1 for i_, st in enumerate(ORDER)}

        def xw(s_, tb):
            if s_ == STAGES - 1:
                return xn2[:, 0, :]
            return xn4[:, tb, :] if s_ == 2 else xn2[:, tb % 2, :]

        def cols8(ap):
            return ap.rearrange("p (a b) -> p a b", a=KT)

        def row_wait(eng, stage, half, tb):
            name, l, nk = stage
            if tb < 3:
                eng.wait_ge(row_full, ROWS.index(stage) * 6 + half * 3 + tb + 1)
            else:
                eng.wait_ge(w_used, W[(name, l, half, nk - 2)] + 1)

        def row_reads(stage, half, tb):
            i = ROWS.index(stage)
            return 4 * half + tb + 1 if i == 0 else 8 + 4 * (i - 1) + tb + 1

        def proj_wait(eng, s_full, name, l, j, mm):
            if mm < 3:
                eng.wait_ge(s_full, 6 * l + 3 * j + mm + 1)
            else:
                eng.wait_ge(w_used, W[(name, l, j)] + 1)

        SECOND_VECS = {"norm_mix", "b_gate", "norm_ffn", "conv_b"}

        def vec_loads(second):
            return sum((VOFF[name] + rows - 1) // P - VOFF[name] // P + 1 for name, rows in VECS if (name in SECOND_VECS) == second)

        def load_vectors(eng, vecs, loaded):
            for name, rows in vecs:
                src = t[{"norm_mix": "norm_mix_2", "b_gate": "b_gate_2", "norm_ffn": "norm_ffn_2",
                         "conv_w": "conv_w_2", "conv_b": "conv_b_2"}.get(name, name)]
                dims = " ".join("abc"[:len(src.shape)])
                src = src.rearrange(f"{dims} -> ({dims})").rearrange("(r n) -> r n", n=P)
                done = 0
                while done < rows:
                    g = VOFF[name] + done
                    m = min(rows - done, P - g % P)
                    eng.dma_start(vstage[g % P:g % P + m, g // P, :], src[done:done + m, :]).then_inc(loaded, 16)
                    done += m

        block = ctx.enter_context(nc.Block())

        def chunk_src(c):
            tensor, key, ps = chunks[c]
            kind = key[0]
            a = t[tensor]
            if kind == "w_in":
                c0 = (key[1] + 2 * key[2]) * P
                return a[0].rearrange("(k p) n -> p k n", p=P)[:, :, c0:c0 + 256], (8, 256)
            if kind == "pool_w":
                return a[0, key[1]].rearrange("(k p) n -> p k n", p=P), (2, 256)
            if kind == "w_branch":
                return a[0, key[1]].rearrange("(k p) n -> p k n", p=P)[:, :, key[2] * 256:key[2] * 256 + 256], (8, 256)
            if kind in ("w_out", "w_out_2", "w_down_2"):
                _, l, half, k0, nk = key
                return a[l or 0].rearrange("(k p) n -> p k n", p=P)[:, k0:k0 + nk, half * 512:half * 512 + 512], (nk, 512)
            if kind in ("w_in_2", "w_in_2v", "w_up_2"):
                _, l, sec = key
                return a[l].rearrange("(k p) n -> p k n", p=P)[:, :, sec * 256:sec * 256 + 256], (8, 256)
            return a[key[1]].rearrange("(k p) n -> p k n", p=P), (2, 1024)

        @block.sync
        def _(sp):
            def chunk_load(c):
                src, (a, b) = chunk_src(c)
                if c >= 2:
                    sp.wait_ge(w_lo, last_piece[c - 2] + 1)
                sp.dma_start(raw[:, c % 2, 0:a * b].rearrange("p (a b) -> p a b", a=a), src).then_inc(raw_in[c % 2], 16)

            xr = t["x"][0].rearrange("(b p) d -> p b d", p=P)
            for tb in range(TB):
                sp.dma_start(x[:, tb, :], xr[:, tb, :]).then_inc(s_x, 16)
            wa = t["w_ada"][0].rearrange("(k p) n -> p k n", p=P)
            sp.wait_ge(s_vec, 16 * vec_loads(False))
            for q in range(8):
                sp.dma_start(ada[:, q, :].rearrange("p (k n) -> p k n", k=KT), wa[:, :, q * 256:(q + 1) * 256]).then_inc(s_ada[q], 16)

            chunk_load(0)
            chunk_load(1)
            for q in range(4):
                if q == 0:
                    sp.wait_ge(s_adsum, 2)
                sp.dma_start(ada[:, q, :].rearrange("p (k n) -> p k n", k=KT), wa[:, :, 2048 + q * 256:2048 + (q + 1) * 256]).then_inc(s_adag, 16)
                chunk_load(2 + q)
            for c in range(6, len(chunks)):
                if chunks[c][0] == "w_out" and chunks[c - 1][0] != "w_out":
                    w_wait_full(sp, ("w_branch", 1, 7))
                    sp.dma_start(lnrow[:, 0, :], t["ln_g"].to_broadcast((P, D))).then_inc(s_ln, 16)
                    sp.dma_start(lnrow[:, 1, :], t["ln_b"].to_broadcast((P, D))).then_inc(s_ln, 16)
                    sp.dma_start(pos_i[:], t["positions_2"].to_broadcast((P, SEQ))).then_inc(s_pos, 16)
                chunk_load(c)
            sp.wait_ge(ff_lo, FT * LAYERS)
            sp.dma_start(frow[:], t["norm_final_2"].rearrange("(a n) -> a n", a=1).to_broadcast((P, D))).then_inc(s_frow, 16)
            ov = out[0].rearrange("(b p) d -> p b d", p=P)
            for tb in range(TB):
                sp.wait_ge(s_xn, 4 * (STAGES - 2) + tb + 1)
                sp.dma_start(ov[:, tb, :], x[:, tb, :]).then_inc(s_out, 16)
            sp.wait_ge(s_out, 16 * TB)

        @block.gpsimd
        def _(pool):
            load_vectors(pool, [v for v in VECS if v[0] in SECOND_VECS], s_vec2)
            nc.gpsimd.memset(neghalf, -0.5).then_inc(pool_chain, 1)
            pool.wait_ge(pool_chain, 1)
            def first_lo(tb):
                pool.wait_ge(h_hi, 8 + tb + 1)
                nc.gpsimd.tensor_tensor(hT[:, 1, :, tb * P:(tb + 1) * P], cols8(xw(2, tb)), hT[:, 0, :, tb * P:(tb + 1) * P].bitcast(F),
                                        ALU.subtract).then_inc(h_lo, 1)

            for i_, (s, tb) in enumerate(ORDER):
                pool.wait_ge(s_ms, i_ + 1)
                nc.gpsimd.tensor_tensor(rstd[:, tb:tb + 1], msq[:, tb:tb + 1], neghalf[:, 0:1], ALU.pow).then_inc(s_rstd, 1)
                if (s, tb) == (1, 3):
                    first_lo(0)
                if s == 2 and tb >= 2:
                    first_lo(tb - 1)
                if (s, tb) == (2, 3):
                    first_lo(3)

        @block.scalar
        def _(act):
            chain = [0]

            def link(ins):
                chain[0] += 1
                ins.then_inc(act_chain, 1)
                act.wait_ge(act_chain, chain[0])

            A = nc.scalar.activation
            act.dma_start(cst[:], t["consts"][:, 0:NKEEP]).then_inc(s_cst, 16)
            act.dma_start(cstage[:], t["consts"][:, NKEEP:NCONST]).then_inc(s_cst, 16)
            load_vectors(act, [v for v in VECS if v[0] not in SECOND_VECS], s_vec)
            act.dma_start(gaterow, t["b_ada"][:, 2048:3072].to_broadcast((P, D))).then_inc(s_bcast, 16)
            act.wait_ge(s_vcol, 1)
            A(cact, vcol[:, VOFF["c"]:VOFF["c"] + 8], ACT.Silu).then_inc(s_cact, 1)
            for w in range(3):
                split_hi(w)
            act.wait_ge(s_modc, 1)
            act.wait_ge(s_xT, 4)
            for ct in range(KT):
                A(hT[:, 0, ct, :], bank(ct), ACT.Identity, bias=modc[:, ct:ct + 1], scale=modc[:, 8 + ct:9 + ct]).then_inc(h_hi, 1)

            def pair_step(p, key, j):
                tt = 2 * p + j
                sec = key[1] // 8 * 8 if key[0] == "w_in" else None
                b = W_BANK[key]
                bias = col("b_in", key[1]) if sec is not None else None
                if sec in (CB, CG, AV, AG, BC, BG):
                    w_wait_full(act, key)
                if sec == CB:
                    if p:
                        act.wait_ge(hc_done, tt - 1)
                    A(glu[:, j, CF_TAPS - 1:], bank(b), ACT.Tanh, bias=halfb[:, key[1]:key[1] + 1], scale=0.5).then_inc(act_read, 1)
                elif sec == CG:
                    A(cg[:, tt, :], bank(b), ACT.Silu, bias=bias).then_inc(act_read, 1)
                elif sec == AV:
                    if tt:
                        act.wait_ge(pooled_lo, tt)
                    A(vpad[:, 16:], bank(b), ACT.Identity, bias=bias).then_inc(act_read, 1)
                elif sec == AG:
                    if key == ("w_in", AG):
                        act.wait_ge(s_gsum, 2)
                    A(sag[:, tt, :], bank(b), ACT.Silu, bias=bias).then_inc(act_read, 1)
                elif sec == BC:
                    A(ybf[:, tt, :], bank(b), ACT.Identity, bias=bias).then_inc(act_read, 1)
                elif sec == BG:
                    A(sbg[:, j, :], bank(b), ACT.Silu, bias=bias).then_inc(act_read, 1)

            def pooled_split(tt):
                act.wait_ge(pooled_f, tt + 1)
                if tt >= 2:
                    w_wait_full(act, ("pool_w", tt // 2 - 1))
                A(poolhl[:, tt % 2, 0, :], vpad[:, 16:], ACT.Copy).then_inc(pooled_hi, 1)

            act.wait_ge(s_ini, SETUP)
            for p in range(4):
                for key in PAIR_KEYS(p):
                    w = W[key]
                    split_hi(w + 3)
                    j = key[1] % 2
                    if key[0] == "pool_w":
                        for jj in range(2):
                            tt = 2 * p + jj
                            act.wait_ge(ya_f, tt + 1)
                            A(yahl[:, 0, tt, :], yaf[:, 0:SEQ], ACT.Copy).then_inc(ya_hi, 1)
                        continue
                    pair_step(p, key, j)
                    if key[0] == "w_in" and key[1] // 8 * 8 == AV:
                        pooled_split(2 * p + j)

            def gate_tanh(key, dst):
                w_wait_full(act, key)
                A(dst, bank(W_BANK[key]), ACT.Tanh, bias=halfb[:, key[1]:key[1] + 1], scale=0.5).then_inc(act_read, 1)

            def mixture_hi(m):
                act.wait_ge(m_part, 8 + m + 1)
                A(mhi[:, m, :], mT[:, m, :], ACT.Copy).then_inc(m_hi, 1)

            for i in range(3):
                for q in range(4):
                    for j in range(2):
                        m = 2 * q + j
                        key = ("w_in", MG + 8 * i + m)
                        split_hi(W[key] + 3)
                        if i == 0 and m == 0:
                            act.wait_ge(hc_done, KT)
                            act.wait_ge(ya_lo, KT)
                        if i == 1 and m == 0:
                            w_wait_full(act, ("w_branch", 0, 7))
                            for k in range(KT):
                                A(ybhi[:, k, :], ybf[:, k, :], ACT.Copy).then_inc(yb_hi, 1)
                        if i == 1 and m == 3:
                            for k in range(KT):
                                act.wait_ge(cen, k + 1)
                                A(sq[:, k, :], hc[:, k, :], ACT.Square).then_inc(sqd, 1)
                        if i == 1 and m == 5:
                            act.wait_ge(ve, 1)
                            A(sq[:, 0, :], sq[:, 0, :], ACT.Sqrt).then_inc(sqr, 1)
                        if i == 1 and m == 6:
                            for k in range(KT):
                                act.wait_ge(nrm, k + 1)
                                A(hc[:, k, :], hc[:, k, :], ACT.Silu, bias=col("cf_ln_b", k), scale=col("cf_ln_g", k)).then_inc(ycs, 1)
                        if i == 1 and m == 7:
                            for k in range(KT):
                                act.wait_ge(ycf, k + 1)
                                A(ychi[:, k, :], hc[:, k, :], ACT.Copy).then_inc(yc_hi, 1)
                        if i == 2:
                            if m:
                                act.wait_ge(m_part, 8 + m - 1)
                            gate_tanh(key, tg2[:, m % 2, :])
                    for j in range(2):
                        m = 2 * q + j
                        split_hi(W[("w_branch", i, m)] + 3)
                        if i < 2:
                            if i and m:
                                act.wait_ge(m_part, m)
                            gate_tanh(("w_in", MG + 8 * i + m), mT[:, m, :] if i == 0 else tg[:])
                        elif m:
                            mixture_hi(m - 1)
            mixture_hi(KT - 1)

            def lead(keys):
                for key in keys:
                    split_hi(W[key] + 3)

            lead(lead_keys(ROWS[0]))
            act.wait_ge(s_rt, 1)
            act.wait_ge(row_read, 4)
            A(table[:, 0, :], rt[:, 0, :], ACT.Sin).then_inc(s_tab, 1)
            act.wait_ge(s_rt, 2)
            A(rt[:, 1, :], rt[:, 1, :], ACT.Sin).then_inc(s_tab, 1)

            def norm_sum(s, tb):
                act.wait_ge(x_ready, 4 * (s - 2) + tb + 1)
                if s == STAGES - 1:
                    if tb:
                        act.wait_ge(s_ssq, 4 * (s - 2) + tb)
                elif s > 2 and tb >= 2:
                    act.wait_ge(h_lo, 8 + 4 * (s - 2) + tb - 1)
                A(xw(s, tb), x[:, tb, :], ACT.Square, accum_out=ssq[:, tb:tb + 1]).then_inc(s_ssq, 1)

            def scaled(s, tb):
                act.wait_ge(s_rstd, root_at[s, tb])
                A(xw(s, tb), x[:, tb, :], ACT.Copy, scale=rstd[:, tb:tb + 1]).then_inc(s_xn, 1)

            def norm_hi(s, tb):
                act.wait_ge(h_f, 4 * (s - 2) + tb + 1)
                A(hT[:, 0, :, tb * P:(tb + 1) * P], cols8(xw(s, tb)), ACT.Copy).then_inc(h_hi, 1)

            def norm(s):
                w0 = resident(ROWS[s - 2])
                norm_sum(s, 0)
                scaled(s, 0)
                norm_sum(s, 1)
                scaled(s, 1)
                if s == 2:
                    norm_sum(s, 2)
                    split_hi(w0 + 4)
                    split_hi(w0 + 5)
                    norm_hi(s, 0)
                    scaled(s, 2)
                    norm_hi(s, 1)
                    norm_sum(s, 3)
                    norm_hi(s, 2)
                    scaled(s, 3)
                else:
                    norm_hi(s, 0)
                    norm_sum(s, 2)
                    scaled(s, 2)
                    norm_hi(s, 1)
                    split_hi(w0 + 4)
                    split_hi(w0 + 5)
                    norm_sum(s, 3)
                    scaled(s, 3)
                    norm_hi(s, 2)
                split_hi(w0 + 6)
                split_hi(w0 + 7)
                norm_hi(s, 3)

            for l in range(LAYERS):
                s = 2 + 2 * l
                norm(s)
                nc.scalar.preload_act_table_set("natural_log_exp_and_others")
                for name, dst, sc in (("sq", sbq, HEAD ** -0.5), ("sk", sbk, 1.0)):
                    for j in range(2):
                        key = (name, l, j)
                        if key != ("sq", l, 0):
                            split_hi(W[key] + 3)
                        w_wait_full(act, key)
                        A(dst[:, j, :], bank(W_BANK[key]), ACT.Copy, scale=sc).then_inc(act_read, 1)
                for j in range(2):
                    key = ("sv", l, j)
                    split_hi(W[key] + 3)
                w_wait_full(act, key)
                b = W_BANK[key]
                A(sbv[:].rearrange("p a b -> p (a b)"), psum[:, b * SEQ:(b + 2) * SEQ], ACT.Copy).then_inc(act_read, 1)

                def sb_logs(h):
                    for kb in range(TB):
                        act.wait_ge(z_ps, 4 * (4 * l + h) + kb + 1)
                        A(sbl[:, SBO[kb]:SBO[kb + 1]], bank(2 + kb)[:, 0:SBO[kb + 1] - SBO[kb]], ACT.Abs).then_inc(sb_abs, 1)
                    for kb in range(TB):
                        act.wait_ge(sb_abs, 4 * (4 * l + h) + kb + 1)
                        v = sbl[:, SBO[kb]:SBO[kb + 1]]
                        A(v, v, ACT.Exp, scale=-1.0).then_inc(act_chain, 1)
                    chain[0] += 4
                    for kb in range(TB):
                        act.wait_ge(act_chain, chain[0] - 3 + kb)
                        v = sbl[:, SBO[kb]:SBO[kb + 1]]
                        A(v, v, ACT.Ln, bias=1.0).then_inc(sb_l, 1)

                def sb_hi(h):
                    act.wait_ge(sp_ready, 4 * (4 * l + h) + 4)
                    A(sphi[:], sbs[:], ACT.Copy).then_inc(sp_hi, 1)

                def sb_exp(h):
                    for kb in range(TB):
                        act.wait_ge(e_ps, 4 * (4 * l + h) + kb + 1)
                        if kb == 0 and h:
                            act.wait_ge(sbo_ps, 4 * l + h)
                        A(sba[:, SBO[kb]:SBO[kb + 1]], bank(2 + kb)[:, 0:SBO[kb + 1] - SBO[kb]], ACT.Exp).then_inc(sb_attn, 1)

                def sb_out(h):
                    act.wait_ge(sbo_ps, 4 * l + h + 1)
                    po = h % 2 * HEAD
                    A(obT[po:po + HEAD, h // 2, 0, :], bank(6)[po:po + HEAD, :], ACT.Copy).then_inc(ob_hi, 1)

                for n_, key in enumerate(DIL_KEYS(l)):
                    split_hi(W[key] + 3)
                    if key[0] in ("dq", "dk"):
                        w_wait_full(act, key)
                        if n_ >= 2:
                            act.wait_ge(rope_done, 12 * l + n_ - 1)
                        A(qhl[:, n_ % 2, 0, :], bank(W_BANK[key]), ACT.Copy, scale=HEAD ** -0.5 if key[0] == "dq" else 1.0)
                        A(qraw[:, n_ % 2, :], bank(W_BANK[key]), ACT.Copy,
                          scale=HEAD ** -0.5 if key[0] == "dq" else 1.0).then_inc(act_read, 1)
                    elif key[3] == 1:
                        w_wait_full(act, key)
                        b = W_BANK[key]
                        A(vd[:, key[2], :, :].rearrange("p a b -> p (a b)"), psum[:, b * SEQ:(b + 2) * SEQ], ACT.Copy).then_inc(act_read, 1)
                    h, ph = n_ // 4, n_ % 4
                    if ph == 0 and h >= 1:
                        sb_out(h - 1)
                    if ph == 0 and h < 4:
                        sb_logs(h)
                    if ph == 1 and h < 4:
                        sb_hi(h)
                    if ph == 2 and h < 4:
                        sb_exp(h)

                def dil_exp(u):
                    act.wait_ge(max_done, 16 * l + u + 1)
                    if u >= 2:
                        act.wait_ge(pT_ps, 16 * l + u - 1)
                    A(prob[:, u % 2, :], psum[:, 2 * SEQ:2 * SEQ + 768], ACT.Exp, bias=nmax[:, u:u + 1],
                      accum_out=den[:, u:u + 1]).then_inc(p_ready, 1)

                def dil_pT(u):
                    act.wait_ge(pT_ps, 16 * l + u + 1)
                    if u >= 2:
                        act.wait_ge(o_ps, 16 * l + u - 1)
                    A(probT[:, u % 2, :], psum[:, 4 * SEQ:4 * SEQ + 768], ACT.Copy).then_inc(pT_ready, 1)

                def dil_oT(r):
                    act.wait_ge(oT_ps, 4 * l + r + 1)
                    A(oaT[:, :, 0, r:SEQ:4], bank(7)[:, 0:256].rearrange("p (a b) -> p a b", a=2), ACT.Copy).then_inc(oa_hi, 1)

                for u in range(16):
                    key = ("gate", l, u)
                    split_hi(W[key] + 3)
                    dil_exp(u)
                    w_wait_full(act, key)
                    A(gates[:, u, :], bank(W_BANK[key]), ACT.Tanh, bias=halfb[:, 96 + 16 * l + u:97 + 16 * l + u], scale=0.5).then_inc(act_read, 1)
                    dil_pT(u)
                    if u % 4 == 3 and u > 4:
                        dil_oT(u // 4 - 1)
                lead([("w_proj_b_2", l, 0), ("w_proj_b_2", l, 1)])
                dil_oT(3)
                lead([("w_proj_a_2", l, 0)])
                for m in range(KT):
                    if m == 4:
                        lead([("w_proj_a_2", l, 1)])
                    act.wait_ge(mix_f, 8 * l + m + 1)
                    A(hT[:, 0, m, :], gates[:, m, :], ACT.Copy).then_inc(mix_hi, 1)
                lead(lead_keys(("w_out_2", l, KT)))
                norm(s + 1)
                for f2 in range(FT // 2):
                    for j in range(2):
                        f = 2 * f2 + j
                        key = ("up_a", l, f)
                        if f:
                            split_hi(W[key] + 3)
                        w_wait_full(act, key)
                        if FT * l + f >= 2:
                            act.wait_ge(fconv, FT * l + f - 1)
                        A(apad[:, j, 2:], bank(W_BANK[key]), ACT.Copy).then_inc(act_read, 1)
                    for j in range(2):
                        f = 2 * f2 + j
                        act.wait_ge(fconv, FT * l + f + 1)
                        if FT * l + f >= 2:
                            act.wait_ge(ff_lo, FT * l + f - 1)
                        A(fsil[:, j, :], facc[:], ACT.Silu).then_inc(silu_done, 1)
                    for j in range(2):
                        f = 2 * f2 + j
                        key = ("up_b", l, f)
                        split_hi(W[key] + 3)
                        await_read(act, key)
                        A(ff[:, f, 0, :], fsil[:, j, :], ACT.Copy).then_inc(ff_hi, 1)
                lead(lead_keys(("w_down_2", l, FT)))
            for tb in range(TB):
                norm_sum(STAGES - 1, tb)

        @block.vector
        def _(dve):
            V = nc.vector
            chain = [0]

            def link(ins):
                chain[0] += 1
                ins.then_inc(dve_chain, 1)
                dve.wait_ge(dve_chain, chain[0])

            def step(ins):
                chain[0] += 1
                ins.then_inc(dve_chain, 1)
                return chain[0]

            V.memset(onesd[:], 1.0 / D).then_inc(s_ini, 1)
            V.memset(negones[:], -1.0).then_inc(s_ini, 1)
            dve.wait_ge(s_cst, 32)
            V.tensor_copy(identb[:], ident).then_inc(s_ini, 1)
            c0 = COFF["band"]
            V.tensor_copy(bandb[:], cstage[:, 0:516]).then_inc(s_ini, 1)
            V.tensor_copy(ownb[:], cstage[:, COFF["own"] - c0:COFF["own"] - c0 + 256]).then_inc(s_ini, 1)
            V.tensor_copy(sbaddb[:], cstage[:, COFF["sbadd"] - c0:COFF["sbadd"] - c0 + P]).then_inc(s_ini, 1)
            def half_stats(tb, half):
                return step(V.bn_stats(bnst[:, (2 * tb + half) * 6:(2 * tb + half) * 6 + 6], x[:, tb, half * 512:(half + 1) * 512]))

            def row_stats(tb):
                link(V.bn_aggr(mv[:, 2 * tb:2 * tb + 2], bnst[:, 12 * tb:12 * tb + 12].rearrange("p (a b) -> p a b", a=2)))
                V.tensor_scalar(msq[:, tb:tb + 1], mv[:, 2 * tb + 1:2 * tb + 2], LN_EPS, None, ALU.add).then_inc(s_ms, 1)

            dve.wait_ge(s_x, 16 * TB)
            for tb in range(TB):
                half_stats(tb, 0)
                dve.wait_ge(dve_chain, half_stats(tb, 1))
                row_stats(tb)
            for tb in range(TB):
                dve.wait_ge(s_rstd, tb + 1)
                V.tensor_scalar(xn1[:, tb, :], x[:, tb, :], mv[:, 2 * tb:2 * tb + 1], rstd[:, tb:tb + 1],
                                ALU.subtract, ALU.mult).then_inc(s_xn, 1)
            dve.wait_ge(s_vT, 6)
            V.tensor_copy(vcol[:, 0:512], bank(0)).then_inc(s_ini, 1)
            V.tensor_copy(vcol[:, 512:NVEC], bank(1)[:, 0:NVEC - 512]).then_inc(s_vcol, 1)
            dve.wait_ge(s_ini, 7)
            dve.wait_ge(s_vcol, 1)
            V.tensor_scalar(halfb[:, 0:96], vcol[:, 0:96], 0.5, None, ALU.mult).then_inc(s_ini, 1)
            V.tensor_scalar(halfb[:, 96:128], vcol[:, VOFF["b_gate"]:VOFF["b_gate"] + 32], 0.5, None, ALU.mult).then_inc(s_ini, 1)

            def summed(g):
                o_ = adsum[:, 2 * g:2 * g + 2, :]
                at_k = lambda k: ada[:, 2 * g:2 * g + 2, k * 256:(k + 1) * 256]
                link(V.tensor_scalar(o_, at_k(0), cact[:, 0:1], None, ALU.mult))
                for k in range(1, KT):
                    ins = V.scalar_tensor_tensor(o_, at_k(k), cact[:, k:k + 1], o_, ALU.mult, ALU.add)
                    if k < KT - 1:
                        link(ins)
                return ins

            dve.wait_ge(s_cact, 1)
            for g in range(4):
                dve.wait_ge(s_ada[2 * g], 16)
                dve.wait_ge(s_ada[2 * g + 1], 16)
                summed(g).then_inc(s_adsum, 1)
            dve.wait_ge(s_mod, 1)
            link(V.tensor_tensor(modc, vcol[:, VOFF["b_ada"]:VOFF["b_ada"] + 16], bank(7)[:, 0:16], ALU.subtract))
            V.tensor_scalar(modc[:, 8:16], modc[:, 8:16], 1.0, None, ALU.add).then_inc(s_modc, 1)
            for w in range(3):
                split_lo(w)
            dve.wait_ge(s_xT, 4)
            dve.wait_ge(s_modc, 1)
            modulated = {}

            def u_lo(ct):
                dve.wait_ge(dve_chain, modulated[ct])
                V.tensor_tensor(hT[:, 1, ct, :], utmp[:, ct % 2, :], hT[:, 0, ct, :].bitcast(F), ALU.subtract).then_inc(h_lo, 1)

            for ct in range(KT):
                dve.wait_ge(h_hi, ct + 1)
                if ct >= 2:
                    dve.wait_ge(h_lo, ct - 1)
                modulated[ct] = step(V.tensor_scalar(utmp[:, ct % 2, :], bank(ct), modc[:, 8 + ct:9 + ct], modc[:, ct:ct + 1], ALU.mult, ALU.add))
                if ct:
                    u_lo(ct - 1)
            u_lo(KT - 1)
            dve.wait_ge(h_lo, KT)
            V.memset(glu[:, :, 0:CF_TAPS - 1], 0.0).then_inc(s_ini, 1)
            V.memset(vpad[:, 0:16], 0.0).then_inc(s_ini, 1)

            conv = []

            def conv_start(tt):
                g = glu[:, tt % 2, :]
                steps = []

                def first(dst, k, bias):
                    def go():
                        if dst is acc1 and tt:
                            dve.wait_ge(hc_done, tt)
                        if bias is not None:
                            last[dst is acc1] = step(V.tensor_scalar(A_(dst), g[:, k:k + SEQ], col("cf_w", 8 * k + tt), bias, ALU.mult, ALU.add))
                        else:
                            last[dst is acc1] = step(V.tensor_scalar(A_(dst), g[:, k:k + SEQ], col("cf_w", 8 * k + tt), None, ALU.mult))
                    return go

                def A_(dst):
                    return acc1[:] if dst is acc1 else hc[:, tt, :]

                last = {False: 0, True: 0}

                def tap(dst, k):
                    def go():
                        dve.wait_ge(dve_chain, last[dst is acc1])
                        last[dst is acc1] = step(V.scalar_tensor_tensor(A_(dst), g[:, k:k + SEQ], col("cf_w", 8 * k + tt), A_(dst), ALU.mult, ALU.add))
                    return go

                def finish():
                    dve.wait_ge(dve_chain, max(last.values()))
                    V.tensor_tensor(hc[:, tt, :], hc[:, tt, :], acc1[:], ALU.add).then_inc(hc_done, 1)

                steps.append(first(hc, 0, col("cf_b", tt)))
                steps.append(first(acc1, 1, None))
                for k in range(2, CF_TAPS):
                    steps.append(tap(acc1 if k % 2 else hc, k))
                steps.append(finish)
                conv.extend(steps)

            def conv_run(n_):
                for _ in range(min(n_, len(conv))):
                    conv.pop(0)()

            def pair_step(p, key, j):
                tt = 2 * p + j
                if key[0] == "pool_w":
                    for jj in range(2):
                        tt = 2 * p + jj
                        w_wait_full(dve, key)
                        if jj == 0:
                            await_read(dve, ("w_in", AG + 2 * p + 1))
                        if tt:
                            dve.wait_ge(ya_lo, tt)
                        V.scalar_tensor_tensor(yaf[:, 0:SEQ], bank(POOL_BANK[tt % 2]), col("pool_scale", tt), sag[:, tt, :],
                                               ALU.mult, ALU.mult).then_inc(ya_f, 1)
                        dve.wait_ge(ya_hi, tt + 1)
                        V.tensor_tensor(yahl[:, 1, tt, :], yaf[:, 0:SEQ], yahl[:, 0, tt, :].bitcast(F), ALU.subtract).then_inc(ya_lo, 1)
                    return
                sec = key[1] // 8 * 8
                if sec == CB:
                    await_read(dve, key)
                    w_wait_full(dve, ("w_in", CA + tt))
                    gl = glu[:, j, CF_TAPS - 1:]
                    link(V.tensor_scalar(gl, gl, 0.5, 0.5, ALU.mult, ALU.add))
                    k_ = W_BANK[("w_in", CA + tt)]
                    V.scalar_tensor_tensor(gl, bank(k_), col("b_in", CA + tt), gl, ALU.add, ALU.mult).then_inc(dve_read, 1)
                    await_read(dve, ("w_in", CA + tt))
                    conv_start(tt)
                elif sec == AV:
                    await_read(dve, key)
                    if p:
                        w_wait_full(dve, ("pool_w", p - 1))
                    src, w_ = vpad, 1
                    for n_ in range(p + 1):
                        dst = sbuf1[:, j, :] if n_ % 2 == 0 else yaf[:]
                        lo_ = 2 ** (n_ + 1)
                        s_ = src[:] if src is vpad else src
                        link(V.tensor_tensor(dst[:, lo_:16 + SEQ], s_[:, lo_:16 + SEQ], s_[:, lo_ - w_:16 + SEQ - w_], ALU.add))
                        src, w_ = dst, w_ * 2
                    link(V.tensor_tensor(src[:, 16:32], src[:, 16:32], cst[:, COFF["corr"] + 16 * p:COFF["corr"] + 16 * p + 16], ALU.mult))
                    V.scalar_tensor_tensor(vpad[:, 16:], src[:, 16:16 + SEQ], 1.0 / w_, vpad[:, 16:], ALU.mult, ALU.subtract).then_inc(pooled_f, 1)
                    dve.wait_ge(pooled_hi, tt + 1)
                    V.tensor_tensor(poolhl[:, j, 1, :], vpad[:, 16:], poolhl[:, j, 0, :].bitcast(F), ALU.subtract).then_inc(pooled_lo, 1)
                elif sec == BH:
                    if j == 0:
                        link(V.memset(yaf[:, 0:2], 0.0))
                    w_wait_full(dve, key)
                    await_read(dve, ("w_in", BC + tt))
                    V.scalar_tensor_tensor(yaf[:, 2:2 + SEQ], bank(W_BANK[key]), col("b_in", key[1]), ybf[:, tt, :],
                                           ALU.add, ALU.mult).then_inc(dve_read, 1)
                    await_read(dve, key)
                    y = ybf[:, tt, :]
                    link(V.tensor_scalar(y, yaf[:, 2:2 + SEQ], col("sc_w", 16 + tt), col("sc_b", tt), ALU.mult, ALU.add))
                    link(V.scalar_tensor_tensor(y, yaf[:, 1:1 + SEQ], col("sc_w", 8 + tt), y, ALU.mult, ALU.add))
                    step(V.scalar_tensor_tensor(y, yaf[:, 0:SEQ], col("sc_w", tt), y, ALU.mult, ALU.add))
                    b_conv[tt] = chain[0]
                elif sec == BB:
                    w_wait_full(dve, key)
                    dve.wait_ge(dve_chain, b_conv[tt])
                    y = ybf[:, tt, :]
                    V.scalar_tensor_tensor(y, bank(W_BANK[key]), col("b_in", key[1]), y, ALU.add, ALU.mult).then_inc(dve_read, 1)
                elif sec == BG:
                    await_read(dve, key)
                    await_read(dve, ("w_in", BB + tt))
                    y = ybf[:, tt, :]
                    V.tensor_tensor(y, y, sbg[:, j, :], ALU.mult).then_inc(yb_f, 1)

            b_conv = {}
            dve.wait_ge(s_ini, SETUP)
            for p in range(4):
                for key in PAIR_KEYS(p):
                    if key == ("w_in", AG + 1):
                        dve.wait_ge(s_gp, 1)
                        dve.wait_ge(s_bcast, 16)
                        V.tensor_tensor(gaterow, gaterow, psum[:, 6 * SEQ:8 * SEQ], ALU.subtract).then_inc(s_gate, 1)
                        dve.wait_ge(s_gate, 1)
                        step(V.tensor_scalar(gaterow, gaterow, 0.5, None, ALU.mult))
                    split_lo(W[key] + 3)
                    pair_step(p, key, key[1] % 2)
                    if key in (("w_in", CG + 1), ("w_in", AV)):
                        g = int(key == ("w_in", AV))
                        dve.wait_ge(s_mod, 1)
                        dve.wait_ge(s_adag, 64)
                        summed(g).then_inc(s_gsum, 1)
                    if key not in (("w_in", CG + 1), ("w_in", AV), ("w_in", AV + 1), ("w_in", AG)):
                        conv_run({AV: 1, AG: 4, BH: 3}.get(key[1] // 8 * 8, 5) if key[0] == "w_in" else 5)

            def mixture_lo(m):
                dve.wait_ge(m_hi, m + 1)
                V.tensor_tensor(mlo[:, m, :], mT[:, m, :], mhi[:, m, :].bitcast(F), ALU.subtract).then_inc(m_lo, 1)

            def yb_split(k):
                dve.wait_ge(yb_hi, k + 1)
                V.tensor_tensor(yblo[:, k, :], ybf[:, k, :], ybhi[:, k, :].bitcast(F), ALU.subtract).then_inc(yb_lo, 1)

            for i in range(3):
                for q in range(4):
                    for j in range(2):
                        m = 2 * q + j
                        split_lo(W[("w_in", MG + 8 * i + m)] + 3)
                        if i == 0:
                            conv_run(6)
                        if i == 1 and m == 0:
                            for k in range(KT):
                                yb_split(k)
                        if i == 1 and m == 3:
                            dve.wait_ge(mean_ps, 1)
                            for k in range(KT):
                                V.tensor_tensor(hc[:, k, :], hc[:, k, :], bank(STAT_BANK), ALU.subtract).then_inc(cen, 1)
                        if i == 1 and m == 5:
                            dve.wait_ge(var_ps, 1)
                            V.tensor_scalar(sq[:, 0, :], bank(STAT_BANK), LN_EPS, None, ALU.add).then_inc(ve, 1)
                            dve.wait_ge(sqr, 1)
                            link(V.reciprocal(sq[:, 0, :], sq[:, 0, :]))
                            dve.wait_ge(cen, KT)
                            for k in range(KT):
                                V.tensor_tensor(hc[:, k, :], hc[:, k, :], sq[:, 0, :], ALU.mult).then_inc(nrm, 1)
                        if i == 1 and m == 7:
                            for k in range(KT):
                                dve.wait_ge(ycs, k + 1)
                                V.tensor_tensor(hc[:, k, :], hc[:, k, :], cg[:, k, :], ALU.mult).then_inc(ycf, 1)
                            for k in range(KT):
                                dve.wait_ge(yc_hi, k + 1)
                                V.tensor_tensor(yclo[:, k, :], hc[:, k, :], ychi[:, k, :].bitcast(F), ALU.subtract).then_inc(yc_lo, 1)
                    for j in range(2):
                        m = 2 * q + j
                        key = ("w_branch", i, m)
                        split_lo(W[key] + 3)
                        w_wait_full(dve, key)
                        await_read(dve, ("w_in", MG + 8 * i + m))
                        if i == 0:
                            V.scalar_tensor_tensor(mT[:, m, :], mT[:, m, :], 1.0, bank(W_BANK[key]), ALU.add, ALU.mult).then_inc(dve_read, 1)
                            conv_run(6)
                            continue
                        g = tg[:] if i == 1 else tg2[:, m % 2, :]
                        V.scalar_tensor_tensor(g, g, 1.0, bank(W_BANK[key]), ALU.add, ALU.mult).then_inc(dve_read, 1)
                        await_read(dve, key)
                        if i == 2:
                            dve.wait_ge(m_part, m + 1)
                        V.tensor_tensor(mT[:, m, :], mT[:, m, :], g, ALU.add).then_inc(m_part, 1)
                        if i == 2 and m:
                            mixture_lo(m - 1)
                if i == 0:
                    conv_run(len(conv))
            mixture_lo(KT - 1)

            w_wait_full(dve, ("w_branch", 2, 7))
            dve.wait_ge(s_pos, 16)
            link(V.tensor_copy(ang[:], pos_i[:]))
            link(V.tensor_scalar(ang[:], ang[:], freq, None, ALU.mult))
            for n_, quarter in ((0, 0.25), (1, 0.0)):
                turns, arg = rt[:, 2, :], rt[:, n_, :]
                link(V.tensor_scalar(turns, ang[:], 1.0 / TWO_PI, quarter, ALU.mult, ALU.add))
                link(V.tensor_scalar(turns, turns, ROUND, None, ALU.add))
                link(V.tensor_scalar(turns, turns, ROUND, None, ALU.subtract))
                link(V.scalar_tensor_tensor(arg, turns, -TURN[0], ang[:], ALU.mult, ALU.add))
                link(V.scalar_tensor_tensor(arg, turns, -TURN[1], arg, ALU.mult, ALU.add))
                link(V.scalar_tensor_tensor(arg, turns, -TURN[2], arg, ALU.mult, ALU.add))
                link(V.tensor_scalar(arg, arg, 2 * np.pi * quarter, 3.1415925, ALU.add, ALU.min))
                V.tensor_scalar(arg, arg, -3.1415925, None, ALU.max).then_inc(s_rt, 1)

            def row_splits(stage, half, a=0, b=None):
                for key in [key for key in lead_keys(stage) if key[2] == half][a:b]:
                    split_lo(W[key] + 3)

            def mean_square(s, tb):
                dve.wait_ge(s_ssq, 4 * (s - 2) + tb + 1)
                V.tensor_scalar(msq[:, tb:tb + 1], ssq[:, tb:tb + 1], 1.0 / D, LN_EPS, ALU.mult, ALU.add).then_inc(s_ms, 1)

            def last_rows(tb):
                dve.wait_ge(s_rstd, root_at[STAGES - 1, tb])
                V.scalar_tensor_tensor(x[:, tb, :], x[:, tb, :], rstd[:, tb:tb + 1], frow[:], ALU.mult, ALU.mult).then_inc(s_xn, 1)

            def gained(s, tb):
                o_ = VOFF["norm_ffn" if s % 2 else "norm_mix"] + 8 * ((s - 2) // 2)
                gain = vcol[:, o_:o_ + 8].rearrange("p (a b) -> p a b", b=1).to_broadcast((P, KT, P))
                dve.wait_ge(s_xT, 4 * (s - 1) + tb + 1)
                V.tensor_tensor(cols8(xw(s, tb)), cols8(psum[:, 2 * tb * SEQ:(2 * tb + 2) * SEQ]), gain, ALU.mult).then_inc(h_f, 1)

            def norm_lo(s, tb):
                dve.wait_ge(h_hi, 8 + 4 * (s - 2) + tb + 1)
                V.tensor_tensor(hT[:, 1, :, tb * P:(tb + 1) * P], cols8(xw(s, tb)), hT[:, 0, :, tb * P:(tb + 1) * P].bitcast(F),
                                ALU.subtract).then_inc(h_lo, 1)

            first = ROWS[0]
            x_part, centred_rows = {}, {}

            def first_rows(half, tb):
                row_wait(dve, first, half, tb)
                xs = x[:, tb, half * 512:(half + 1) * 512]
                if half or tb >= 2:
                    dve.wait_ge(dve_chain, x_part[half if tb >= 2 else 0, (tb - 2) % TB])
                V.tensor_tensor(prod[:, tb % 2, :], bank(4 * half + tb), gaterow[:, half * 512:(half + 1) * 512], ALU.mult).then_inc(row_read, 1)
                dve.wait_ge(row_read, row_reads(first, half, tb))
                x_part[half, tb] = step(V.scalar_tensor_tensor(xs, xs, ALPHA, prod[:, tb % 2, :], ALU.mult, ALU.add))
                dve.wait_ge(dve_chain, x_part[half, tb])
                half_stats(tb, half)
                if half:
                    dve.wait_ge(dve_chain, chain[0])
                    row_stats(tb)
                    centred_rows[tb] = step(V.scalar_tensor_tensor(x[:, tb, :], x[:, tb, :], mv[:, 2 * tb:2 * tb + 1], lnrow[:, 0, :],
                                                                   ALU.subtract, ALU.mult))

            def first_normed(tb):
                dve.wait_ge(s_rstd, root_at[1, tb])
                dve.wait_ge(dve_chain, centred_rows[tb])
                V.scalar_tensor_tensor(x[:, tb, :], x[:, tb, :], rstd[:, tb:tb + 1], lnrow[:, 1, :], ALU.mult, ALU.add).then_inc(x_ready, 1)

            dve.wait_ge(s_ln, 32)
            row_splits(first, 0)
            for tb in range(TB):
                first_rows(0, tb)
                if tb == 0:
                    row_splits(first, 1)
            w0 = resident(first)
            for tb in range(TB):
                if tb == 3:
                    gained(2, 0)
                first_rows(1, tb)
                if tb == 3:
                    split_lo(w0 + 4)
                    split_lo(w0 + 5)
                if tb:
                    mean_square(2, tb - 1)
                if tb == 3:
                    gained(2, 1)
                first_normed(tb)
            mean_square(2, 3)
            gained(2, 2)
            split_lo(w0 + 6)
            gained(2, 3)
            split_lo(w0 + 7)

            def add_rows(stage, scale):
                s = 2 + ROWS.index(stage)
                last = s == STAGES - 1
                w0 = resident(stage)

                def add(half, tb):
                    row_wait(dve, stage, half, tb)
                    xs = x[:, tb, half * 512:(half + 1) * 512]
                    V.scalar_tensor_tensor(xs, bank(4 * half + tb), scale, xs, ALU.mult, ALU.add)\
                     .then_inc(x_ready if half else row_read, 1)

                row_splits(stage, 0)
                for tb in range(TB):
                    add(0, tb)
                    if tb == 1:
                        row_splits(stage, 1, 0, 1)
                row_splits(stage, 1, 1)
                if last:
                    dve.wait_ge(s_frow, 16)
                for tb in range(TB):
                    if tb == 3:
                        split_lo(w0 + 4)
                    add(1, tb)
                    if tb == 3:
                        split_lo(w0 + 5)
                    mean_square(s, tb)
                    if last:
                        last_rows(tb)
                    elif tb:
                        gained(s, tb - 1)
                        norm_lo(s, tb - 1)
                if not last:
                    split_lo(w0 + 6)
                    gained(s, 3)
                    split_lo(w0 + 7)
                    norm_lo(s, 3)

            for l in range(LAYERS):
                s = 2 + 2 * l
                if l == 0:
                    link(V.tensor_copy(negtri_r[:], negtri))
                    step(V.tensor_copy(swap_r[:], swapm))
                    step(V.tensor_copy(negones_r[:], negones[:]))
                    dve.wait_ge(s_tab, 2)
                    link(V.tensor_scalar(table[:, 1, :], rt[:, 1, :], sign, None, ALU.mult))
                for key in (("sq", l, 1), ("sk", l, 0), ("sk", l, 1), ("sv", l, 0), ("sv", l, 1)):
                    split_lo(W[key] + 3)

                def rope_lo(n_):
                    await_read(dve, DIL_KEYS(l)[n_])
                    V.tensor_tensor(qhl[:, n_ % 2, 1, :], qraw[:, n_ % 2, :], qhl[:, n_ % 2, 0, :].bitcast(F), ALU.subtract).then_inc(q_lo, 1)

                def rope(n_):
                    isq, g, j = n_ < 6, n_ // 2 % 3, n_ % 2
                    await_read(dve, DIL_KEYS(l)[n_])
                    if n_:
                        dve.wait_ge(rope_done, 12 * l + n_)
                    V.tensor_tensor(rot[:, 0, :], qraw[:, n_ % 2, :], table[:, 0, :], ALU.mult).then_inc(dve_chain, 1)
                    chain[0] += 1
                    dve.wait_ge(rot_ps, 12 * l + n_ + 1)
                    link(V.tensor_tensor(rot[:, 1, :], bank(7), table[:, 1, :], ALU.mult))
                    dst = (qd if isq else kd)[:, g, j, :]
                    if isq or g:
                        dst = dst.rearrange("p (r u) -> p u r", r=4)
                        a, b = (rot[:, i_, :].rearrange("p (u r) -> p u r", r=4) for i_ in range(2))
                    else:
                        a, b = rot[:, 0, :], rot[:, 1, :]
                    V.tensor_tensor(dst, a, b, ALU.add).then_inc(rope_done, 1)

                def sb_softplus(h):
                    for kb in range(TB):
                        dve.wait_ge(sb_l, 4 * (4 * l + h) + kb + 1)
                        w_ = SBO[kb + 1] - SBO[kb]
                        v = sbs[:, SBO[kb]:SBO[kb + 1]]
                        link(V.scalar_tensor_tensor(v, bank(2 + kb)[:, 0:w_], 0.0, sbl[:, SBO[kb]:SBO[kb + 1]], ALU.max, ALU.add))
                        v = sbs[:, SBO[kb]:SBO[kb] + P]
                        V.tensor_tensor(v, v, sbmul, ALU.mult).then_inc(sp_ready, 1)

                def sb_lo(h):
                    dve.wait_ge(sp_hi, 4 * l + h + 1)
                    V.tensor_tensor(splo[:], sbs[:], sphi[:].bitcast(F), ALU.subtract).then_inc(sp_lo, 1)

                def sb_out(h):
                    dve.wait_ge(ob_hi, 4 * l + h + 1)
                    po = h % 2 * HEAD
                    V.tensor_tensor(obT[po:po + HEAD, h // 2, 1, :], bank(6)[po:po + HEAD, :],
                                    obT[po:po + HEAD, h // 2, 0, :].bitcast(F), ALU.subtract).then_inc(ob_lo, 1)

                for n_, key in enumerate(DIL_KEYS(l)):
                    split_lo(W[key] + 3)
                    if 1 <= n_ <= 12:
                        rope(n_ - 1)
                    if n_ < 12:
                        rope_lo(n_)
                    h, ph = n_ // 4, n_ % 4
                    if ph == 0 and h >= 1:
                        sb_out(h - 1)
                    if ph == 0 and h < 4:
                        sb_softplus(h)
                    if ph == 1 and h < 4:
                        sb_lo(h)

                def dil_max(u):
                    dve.wait_ge(s_ps, 16 * l + u + 1)
                    link(V.reduce_max(nmax[:, u:u + 1], psum[:, 2 * SEQ:2 * SEQ + 768], AX.X))
                    V.tensor_scalar(nmax[:, u:u + 1], nmax[:, u:u + 1], -1.0, None, ALU.mult).then_inc(max_done, 1)

                def dil_rden(u):
                    dve.wait_ge(p_ready, 16 * l + u + 1)
                    rd[u] = step(V.reciprocal(rden[:, u:u + 1], den[:, u:u + 1]))

                def dil_out(u):
                    r, h = u // 4, u % 4
                    dve.wait_ge(o_ps, 16 * l + u + 1)
                    dve.wait_ge(dve_chain, rd[u])
                    V.tensor_scalar(osb[:, r % 2, h * HEAD:(h + 1) * HEAD], bank(6)[:, 0:HEAD], rden[:, u:u + 1], None, ALU.mult).then_inc(o_ready, 1)

                def dil_oT(r):
                    dve.wait_ge(oa_hi, 4 * l + r + 1)
                    V.tensor_tensor(oaT[:, :, 1, r:SEQ:4], bank(7)[:, 0:256].rearrange("p (a b) -> p a b", a=2),
                                    oaT[:, :, 0, r:SEQ:4].bitcast(F), ALU.subtract).then_inc(oa_lo, 1)

                rd = {}
                for u in range(16):
                    split_lo(W[("gate", l, u)] + 3)
                    dil_max(u)
                    dil_rden(u)
                    if u >= 2:
                        dil_out(u - 2)
                    if u % 4 == 3 and u > 4:
                        dil_oT(u // 4 - 1)
                dil_out(14)
                def mixed_lo(m):
                    dve.wait_ge(mix_hi, 8 * l + m + 1)
                    V.tensor_tensor(hT[:, 1, m, :], gates[:, m, :], hT[:, 0, m, :].bitcast(F), ALU.subtract).then_inc(mix_lo, 1)

                for j in range(2):
                    split_lo(W[("w_proj_b_2", l, j)] + 3)
                    for mm in range(4):
                        m = 4 * j + mm
                        proj_wait(dve, pb_ps, "w_proj_b_2", l, j, mm)
                        if mm == 0:
                            await_read(dve, ("gate", l, 15))
                        V.scalar_tensor_tensor(gates[:, 8 + m, :], gates[:, 8 + m, :], 1.0, bank(m), ALU.add, ALU.mult).then_inc(pb_f, 1)
                dil_out(15)
                dil_oT(3)
                for j in range(2):
                    split_lo(W[("w_proj_a_2", l, j)] + 3)
                    for mm in range(4):
                        m = 4 * j + mm
                        proj_wait(dve, pa_ps, "w_proj_a_2", l, j, mm)
                        V.scalar_tensor_tensor(gates[:, m, :], gates[:, m, :], 1.0, bank(m), ALU.add, ALU.mult).then_inc(pa_f, 1)
                        dve.wait_ge(pa_f, 8 * l + m + 1)
                        V.tensor_tensor(gates[:, m, :], gates[:, m, :], gates[:, 8 + m, :], ALU.add).then_inc(mix_f, 1)
                        if m:
                            mixed_lo(m - 1)
                mixed_lo(KT - 1)
                add_rows(("w_out_2", l, KT), 0.5)

                link(V.memset(apad[:, :, 0:2], 0.0))
                for f2 in range(FT // 2):
                    for j in range(2):
                        f = 2 * f2 + j
                        key = ("up_a", l, f)
                        if f:
                            split_lo(W[key] + 3)
                        await_read(dve, key)
                        if FT * l + f:
                            dve.wait_ge(silu_done, FT * l + f)
                        cw = lambda k: col("conv_w", (3 * l + k) * FT + f)
                        link(V.tensor_scalar(facc[:], apad[:, j, 2:2 + SEQ], cw(2), col("conv_b", FT * l + f), ALU.mult, ALU.add))
                        link(V.scalar_tensor_tensor(facc[:], apad[:, j, 1:1 + SEQ], cw(1), facc[:], ALU.mult, ALU.add))
                        V.scalar_tensor_tensor(facc[:], apad[:, j, 0:SEQ], cw(0), facc[:], ALU.mult, ALU.add).then_inc(fconv, 1)
                    for j in range(2):
                        f = 2 * f2 + j
                        key = ("up_b", l, f)
                        split_lo(W[key] + 3)
                        w_wait_full(dve, key)
                        dve.wait_ge(silu_done, FT * l + f + 1)
                        V.tensor_tensor(fsil[:, j, :], bank(W_BANK[key]), fsil[:, j, :], ALU.mult).then_inc(dve_read, 1)
                        dve.wait_ge(ff_hi, FT * l + f + 1)
                        V.tensor_tensor(ff[:, f, 1, :], fsil[:, j, :], ff[:, f, 0, :].bitcast(F), ALU.subtract).then_inc(ff_lo, 1)
                add_rows(("w_down_2", l, FT), 1.0)

        @block.tensor
        def _(pe):
            M = nc.tensor.matmul
            reader = {}

            def take(*banks):
                for b in banks:
                    if b in reader:
                        pe.wait_ge(*reader.pop(b))

            def give(b, s_, value):
                reader[b] = (s_, value)

            def passes(out_, stat_hi, stat_lo, mov_hi, mov_lo, start, stop, **kw):
                M(out_, stat_hi, mov_hi, start=start, stop=False, **kw)
                M(out_, stat_hi, mov_lo, start=False, stop=False, **kw)
                return M(out_, stat_lo, mov_hi, start=False, stop=stop, **kw)

            def col_tile(key, xhi, xlo, ready=None):
                w = W[key]
                b = W_BANK[key]
                take(b)
                pe.wait_ge(w_lo, w + 1)
                hi, lo = whl_view(w, 0), whl_view(w, 1)
                for k in range(KT):
                    if ready is not None:
                        pe.wait_ge(ready[0], ready[1] + k + 1)
                    ins = passes(bank(b), hi[:, k, :], lo[:, k, :], xhi(k), xlo(k), k == 0, k == KT - 1)
                ins.then_inc(w_used, 1)
                if key in rcount:
                    give(b, *read_of(key))

            def transposed(s, tb):
                pe.wait_ge(s_xn, 4 * (s - 1) + tb + 1)
                take(2 * tb, 2 * tb + 1)
                for ct in range(KT):
                    ins = nc.tensor.transpose(psum[:, 2 * tb * SEQ + ct * P:2 * tb * SEQ + (ct + 1) * P], xw(s, tb)[:, ct * P:(ct + 1) * P], ident)
                ins.then_inc(s_xT, 1)
                give(2 * tb, h_f, 4 * (s - 2) + tb + 1)
                give(2 * tb + 1, h_f, 4 * (s - 2) + tb + 1)

            def row_tiles(stage, xhi, xlo, ready):
                name, l, nk = stage
                s = 2 + ROWS.index(stage)
                lag = 3 if s == 2 else 1

                def block_of(half, tb, k0):
                    w = W[(name, l, half, k0)]
                    pe.wait_ge(w_lo, w + 1)
                    hi, lo = whl_view(w, 0), whl_view(w, 1)
                    ts = slice(tb * P, (tb + 1) * P)
                    for kk in range(2):
                        k = k0 + kk
                        if half == 0 and tb == 0:
                            pe.wait_ge(ready[0], ready[1] + k + 1)
                        ins = passes(bank(4 * half + tb), xhi(k)[:, ts], xlo(k)[:, ts], hi[:, kk, :], lo[:, kk, :],
                                     k == 0, k == nk - 1)
                    if k0 == nk - 2 and tb < 3:
                        ins.then_inc(row_full, 1)
                    if tb == 3:
                        ins.then_inc(w_used, 1)

                for half in range(2):
                    take(*range(4 * half, 4 * half + 4))
                    for k0 in range(0, nk - 8 * half, 2):
                        for tb in range(TB):
                            block_of(half, tb, k0)
                    for tb in range(TB):
                        if half:
                            for k0 in range(nk - 8, nk, 2):
                                block_of(half, tb, k0)
                        if half and l is not None:
                            give(4 * half + tb, x_ready, 4 * ROWS.index(stage) + tb + 1)
                        else:
                            give(4 * half + tb, row_read, row_reads(stage, half, tb))
                        if half and tb >= lag and s < STAGES - 1:
                            transposed(s, tb - lag)
                if lag == 3:
                    transposed(s, 1)
                    transposed(s, 2)

            def first_tiles(keys, s):
                for c0 in (0, SEQ // 2):
                    for i_, key in enumerate(keys):
                        w, b = W[key], W_BANK[key]
                        if c0 == 0:
                            take(b)
                            pe.wait_ge(w_lo, w + 1)
                        if i_ == 0:
                            pe.wait_ge(h_lo, 8 + 4 * (s - 2) + (4 if c0 else 2))
                        hi, lo = whl_view(w, 0), whl_view(w, 1)
                        cs = slice(c0, c0 + SEQ // 2)
                        for k in range(KT):
                            ins = passes(bank(b)[:, cs], hi[:, k, :], lo[:, k, :], hT[:, 0, k, cs], hT[:, 1, k, cs],
                                         k == 0, k == KT - 1, skip_group_check=True)
                        if c0:
                            ins.then_inc(w_used, 1)
                            give(b, *read_of(key))
                        elif i_ == 1:
                            transposed(s, 3)

            h_at = lambda hl: (lambda k: hT[:, hl, k, :])

            pe.wait_ge(s_cst, 32)
            pe.wait_ge(s_vec, 16 * vec_loads(False))
            pe.wait_ge(s_vec2, 16 * vec_loads(True))
            for g in range((NVEC + P - 1) // P):
                rows = min(P, NVEC - g * P)
                o_ = bank(g // 4)[:, g % 4 * P:g % 4 * P + rows]
                nc.tensor.transpose(o_, vstage[0:rows, g, :], ident[0:rows, 0:rows]).then_inc(s_vT, 1)
            give(0, s_ini, 7)
            give(1, s_vcol, 1)
            for tb in range(TB):
                pe.wait_ge(s_xn, tb + 1)
                for ct in range(KT - 1):
                    if tb == 0:
                        take(ct)
                    nc.tensor.transpose(bank(ct)[:, tb * P:(tb + 1) * P], xn1[:, tb, ct * P:(ct + 1) * P], ident)
            pe.wait_ge(s_ini, 2)
            for m in range(16):
                if m % 4 == 0:
                    pe.wait_ge(s_adsum, m // 4 + 1)
                ins = M(bank(7)[:, m:m + 1], adsum[:, m // 2, m % 2 * P:(m % 2 + 1) * P], negones[:, 0:1], start=True, stop=True)
            ins.then_inc(s_mod, 1)
            pe.wait_ge(s_modc, 1)
            for tb in range(TB):
                nc.tensor.transpose(bank(7)[:, tb * P:(tb + 1) * P], xn1[:, tb, (KT - 1) * P:], ident).then_inc(s_xT, 1)
            for ct in range(KT):
                give(ct, h_lo, ct + 1)

            for p in range(4):
                for key in PAIR_KEYS(p):
                    if key[0] == "pool_w":
                        w = W[key]
                        pe.wait_ge(w_lo, w + 1)
                        pe.wait_ge(pooled_lo, 2 * p + 2)
                        take(*POOL_BANK)
                        hi, lo = whl_view(w, 0), whl_view(w, 1)
                        for j in range(2):
                            for k in range(2):
                                ins = passes(bank(POOL_BANK[j]), hi[:, k, j * P:(j + 1) * P], lo[:, k, j * P:(j + 1) * P],
                                             poolhl[:, k, 0, :], poolhl[:, k, 1, :], k == 0, k == 1)
                            give(POOL_BANK[j], ya_f, 2 * p + j + 1)
                        ins.then_inc(w_used, 1)
                        continue
                    col_tile(key, h_at(0), h_at(1), (h_lo, 0) if key == ("w_in", CA) else None)
                    if key == ("w_in", AG):
                        pe.wait_ge(s_gsum, 2)
                        take(6, 7)
                        for q in range(2):
                            ins = M(bank(6 + q), negones[:], adsum[:, 2 * q:2 * q + 2, :].rearrange("p a b -> p (a b)"), start=True, stop=True)
                        ins.then_inc(s_gp, 1)
                        give(6, s_gate, 1)
                        give(7, s_gate, 1)

            operand = [(lambda k: yahl[:, 0, k, :], lambda k: yahl[:, 1, k, :], (ya_lo, 0)),
                       (lambda k: ybhi[:, k, :], lambda k: yblo[:, k, :], (yb_lo, 0)),
                       (lambda k: ychi[:, k, :], lambda k: yclo[:, k, :], (yc_lo, 0))]
            for i in range(3):
                for q in range(4):
                    if i == 1 and q == 1:
                        pe.wait_ge(hc_done, KT)
                        take(STAT_BANK)
                        for k in range(KT):
                            ins = M(bank(STAT_BANK), onesd[:], hc[:, k, :], start=k == 0, stop=k == KT - 1)
                        ins.then_inc(mean_ps, 1)
                        give(STAT_BANK, cen, KT)
                    if i == 1 and q == 2:
                        take(STAT_BANK)
                        for k in range(KT):
                            pe.wait_ge(sqd, k + 1)
                            ins = M(bank(STAT_BANK), onesd[:], sq[:, k, :], start=k == 0, stop=k == KT - 1)
                        ins.then_inc(var_ps, 1)
                        give(STAT_BANK, ve, 1)
                    for j in range(2):
                        col_tile(("w_in", MG + 8 * i + 2 * q + j), h_at(0), h_at(1))
                    for j in range(2):
                        hi_, lo_, ready = operand[i]
                        col_tile(("w_branch", i, 2 * q + j), hi_, lo_, ready if q == 0 and j == 0 else None)
            row_tiles(ROWS[0], lambda k: mhi[:, k, :], lambda k: mlo[:, k, :], (m_lo, 0))

            for l in range(LAYERS):
                s = 2 + 2 * l
                def token_tile(key, strided):
                    w = W[key]
                    b = W_BANK[key]
                    first_, last_ = key[-1] == 0, key[-1] == 1
                    if first_:
                        take(b, b + 1)
                    pe.wait_ge(w_lo, w + 1)
                    hi, lo = whl_view(w, 0), whl_view(w, 1)
                    for tb in range(TB):
                        ts = slice(tb, SEQ, 4) if strided else slice(tb * P, (tb + 1) * P)
                        o_ = bank(b + tb // 2)[:, tb % 2 * 256:tb % 2 * 256 + 256]
                        for kk in range(4):
                            k = 4 * key[-1] + kk
                            ins = passes(o_, hT[:, 0, k, ts], hT[:, 1, k, ts], hi[:, kk, :], lo[:, kk, :],
                                         k == 0 and tb % 2 == 0, last_ and kk == 3, skip_group_check=True)
                    ins.then_inc(w_used, 1)
                    if last_:
                        give(b, *read_of(key))
                        give(b + 1, *read_of(key))

                first_tiles([("sq", l, 0), ("sq", l, 1), ("sk", l, 0), ("sk", l, 1)], s)
                token_tile(("sv", l, 0), False)
                token_tile(("sv", l, 1), False)

                def sb_scores(h):
                    po = h % 2 * HEAD
                    rows = slice(po, po + HEAD)
                    await_read(pe, ("sq", l, 1))
                    await_read(pe, ("sk", l, 1))
                    for kb in range(TB):
                        take(2 + kb)
                        M(bank(2 + kb)[:, 0:SEQ - kb * P], sbk[rows, h // 2, kb * P:(kb + 1) * P], sbq[rows, h // 2, kb * P:],
                          start=True, stop=True, skip_group_check=True).then_inc(z_ps, 1)

                def sb_exponents(h):
                    for kb in range(TB):
                        n0 = 4 * (4 * l + h)
                        if kb == 0:
                            pe.wait_ge(sp_lo, 4 * l + h + 1)
                        for jb in range(kb, TB):
                            for part in (sphi, splo):
                                M(bank(2 + kb)[:, (jb - kb) * P:SEQ - kb * P], (negtri_r if jb == kb else negones_r)[:],
                                  part[:, SBO[jb]:SBO[jb + 1]], start=False, stop=False, skip_group_check=True)
                        M(bank(2 + kb)[:, 0:P], identb[:], sbaddb[:], start=False, stop=True, skip_group_check=True).then_inc(e_ps, 1)
                        give(2 + kb, sb_attn, n0 + kb + 1)

                def sb_values(h):
                    po = h % 2 * HEAD
                    take(6)
                    if h == 0:
                        await_read(pe, ("sv", l, 1))
                    for kb in range(TB):
                        pe.wait_ge(sb_attn, 4 * (4 * l + h) + kb + 1)
                        ins = M(bank(6)[po:po + HEAD, kb * P:], sbv[:, kb, h * HEAD:(h + 1) * HEAD], sba[:, SBO[kb]:SBO[kb + 1]],
                                start=kb == 0, stop=kb == TB - 1, skip_group_check=True)
                    ins.then_inc(sbo_ps, 1)
                    give(6, ob_lo, 4 * l + h + 1)

                for n_, key in enumerate(DIL_KEYS(l)):
                    if key[0] == "dv":
                        token_tile(key, key[2] > 0)
                    else:
                        col_tile(key, h_at(0), h_at(1))
                    if 1 <= n_ <= 12:
                        pe.wait_ge(q_lo, 12 * l + n_)
                        take(7)
                        M(bank(7), swap_r[:], qhl[:, (n_ - 1) % 2, 0, :], start=True, stop=False)
                        M(bank(7), swap_r[:], qhl[:, (n_ - 1) % 2, 1, :], start=False, stop=True).then_inc(rot_ps, 1)
                        give(7, rope_done, 12 * l + n_)
                    h, ph = n_ // 4, n_ % 4
                    if ph == 0 and h >= 1:
                        sb_values(h - 1)
                    if ph == 0 and h < 4:
                        sb_scores(h)
                    if ph == 2 and h < 4:
                        sb_exponents(h)

                def dil_scores(u):
                    r, h = u // 4, u % 4
                    po = h % 2 * HEAD
                    rows = slice(po, po + HEAD)
                    if u == 0:
                        pe.wait_ge(rope_done, 12 * l + 12)
                    take(2, 3)
                    for g in range(3):
                        o_ = psum[:, 2 * SEQ:3 * SEQ] if g == 0 else psum[:, 3 * SEQ + (g - 1) * P:3 * SEQ + g * P]
                        keys = kd[rows, 0, h // 2, :] if g == 0 else kd[rows, g, h // 2, r * P:(r + 1) * P]
                        mask = bandb[:, 3 - r:3 - r + SEQ] if g == 0 else ownb[:, (g - 1) * P:g * P]
                        M(o_, qd[rows, g, h // 2, r * P:(r + 1) * P], keys, start=True, stop=False)
                        ins = M(o_, identb[:], mask, start=False, stop=True)
                    ins.then_inc(s_ps, 1)
                    give(2, p_ready, 16 * l + u + 1)
                    give(3, p_ready, 16 * l + u + 1)

                def dil_transposes(u):
                    pe.wait_ge(p_ready, 16 * l + u + 1)
                    take(4, 5)
                    for b in range(6):
                        ins = nc.tensor.transpose(psum[:, 4 * SEQ + b * P:4 * SEQ + (b + 1) * P], prob[:, u % 2, b * P:(b + 1) * P], ident)
                    ins.then_inc(pT_ps, 1)
                    give(4, pT_ready, 16 * l + u + 1)
                    give(5, pT_ready, 16 * l + u + 1)

                def dil_values(u):
                    r, h = u // 4, u % 4
                    if u == 0:
                        await_read(pe, ("dv", l, 2, 1))
                    pe.wait_ge(pT_ready, 16 * l + u + 1)
                    take(6)
                    hs = slice(h * HEAD, (h + 1) * HEAD)
                    vals = [vd[:, 0, b, hs] for b in range(TB)] + [vd[:, 1, r, hs], vd[:, 2, r, hs]]
                    for b, v in enumerate(vals):
                        ins = M(bank(6)[:, 0:HEAD], probT[:, u % 2, b * P:(b + 1) * P], v, start=b == 0, stop=b == 5)
                    ins.then_inc(o_ps, 1)
                    give(6, o_ready, 16 * l + u + 1)

                def dil_oT(r):
                    pe.wait_ge(o_ready, 16 * l + 4 * r + 4)
                    take(7)
                    for ct in range(2):
                        ins = nc.tensor.transpose(bank(7)[:, ct * P:(ct + 1) * P], osb[:, r % 2, ct * P:(ct + 1) * P], ident)
                    ins.then_inc(oT_ps, 1)
                    give(7, oa_lo, 4 * l + r + 1)

                dil_scores(0)
                for u in range(16):
                    col_tile(("gate", l, u), h_at(0), h_at(1))
                    dil_transposes(u)
                    if u < 15:
                        dil_scores(u + 1)
                    if u:
                        dil_values(u - 1)
                    if u % 4 == 2 and u > 4:
                        dil_oT(u // 4 - 1)

                def projection(name, oT, s_full, s_read):
                    for j in range(2):
                        w = W[(name, l, j)]
                        pe.wait_ge(w_lo, w + 1)
                        hi, lo = whl_view(w, 0), whl_view(w, 1)
                        for mm in range(4):
                            m = 4 * j + mm
                            take(m)
                            for k in range(2):
                                ins = passes(bank(m), hi[:, k, mm * P:(mm + 1) * P], lo[:, k, mm * P:(mm + 1) * P],
                                             oT[:, k, 0, :], oT[:, k, 1, :], k == 0, k == 1)
                            if mm < 3:
                                ins.then_inc(s_full, 1)
                            give(m, s_read, 8 * l + m + 1)
                        ins.then_inc(w_used, 1)

                pe.wait_ge(ob_lo, 4 * l + 4)
                projection("w_proj_b_2", obT, pb_ps, pb_f)
                dil_values(15)
                dil_oT(3)
                pe.wait_ge(oa_lo, 4 * l + 4)
                projection("w_proj_a_2", oaT, pa_ps, pa_f)
                row_tiles(("w_out_2", l, KT), h_at(0), h_at(1), (mix_lo, 8 * l))
                first_tiles([(name, l, j) for name in ("up_a", "up_b") for j in range(2)], s + 1)
                for f2 in range(1, FT // 2):
                    for name in ("up_a", "up_b"):
                        for j in range(2):
                            col_tile((name, l, 2 * f2 + j), h_at(0), h_at(1))
                row_tiles(("w_down_2", l, FT), lambda k: ff[:, k, 0, :], lambda k: ff[:, k, 1, :], (ff_lo, FT * l))


_INS = ["x", "c", "w_ada", "b_ada", "w_in", "b_in", "pool_w", "pool_scale", "sc_w", "sc_b", "cf_w", "cf_b", "cf_ln_g",
        "cf_ln_b", "w_branch", "w_out", "ln_g", "ln_b", "positions_2", "norm_mix_2", "w_in_2", "b_gate_2", "w_proj_a_2",
        "w_proj_b_2", "w_out_2", "norm_ffn_2", "w_up_2", "conv_w_2", "conv_b_2", "w_down_2", "norm_final_2"]


def kernel(**inputs):
    import concourse.bacc as bacc
    from concourse.bass_utils import run_bass_kernel_spmd

    nc = bacc.Bacc("TRN2", target_bir_lowering=False, num_devices=1)
    arrays = {f"in_{name}": np.ascontiguousarray(inputs[name]) for name in _INS}
    arrays["in_consts"] = shape_constants()
    t = {name[3:]: nc.dram_tensor(name, a.shape, mybir.dt.from_np(a.dtype), kind="ExternalInput").ap() for name, a in arrays.items()}
    out = nc.dram_tensor("out", (1, SEQ, D), mybir.dt.float32, kind="ExternalOutput").ap()
    build(nc, t, out)
    r = run_bass_kernel_spmd(nc, [arrays], core_ids=[0])
    return r.results[0]["out"]
```
